# Optimizing a Trainium2 kernel written in Bass

```python
import math
import jax, jax.numpy as jnp
from jax import lax
import numpy as np

D_MODEL = 2048
BATCH = 1
SEQ = 256
DEPTH = 1

SSM_WIDTH = D_MODEL // 2
SSM_GROUP = 16
SSM_GROUPS = SSM_WIDTH // SSM_GROUP
SSM_STATE = 64
DT_MIN = 0.001
DT_MAX = 0.1
ATTN_HEADS = 8
HEAD_DIM = 128
ATTN_WIDTH = ATTN_HEADS * HEAD_DIM
MOBA_BLOCK = 256
MOBA_TOPK = 3
Q_BLOCK = 128
REL_BUCKETS = 32
REL_MAX_DIST = 128
D_FF = 4 * D_MODEL
N_MOD = 6
EPS = 1e-6
NEG_INF = -1e30
IN_WIDTH = SSM_WIDTH + 3 * ATTN_WIDTH + 2 * D_MODEL


def rms_norm(x, g):
    x32 = x.astype(jnp.float32)
    y = x32 * lax.rsqrt(jnp.mean(x32 * x32, axis=-1, keepdims=True) + EPS)
    return (y * g.astype(jnp.float32)).astype(x.dtype)

def _ssm_combine(lhs, rhs):
    a_re1, a_im1, b_re1, b_im1 = lhs
    a_re2, a_im2, b_re2, b_im2 = rhs
    a_re = a_re2 * a_re1 - a_im2 * a_im1
    a_im = a_re2 * a_im1 + a_im2 * a_re1
    b_re = a_re2 * b_re1 - a_im2 * b_im1 + b_re2
    b_im = a_re2 * b_im1 + a_im2 * b_re1 + b_im2
    return (a_re, a_im, b_re, b_im)

def s5_branch(u, a_re, a_im, log_dt, b_re, b_im, c_re, c_im, d_skip, w_glu, b_glu):
    bsz, seq_len, _ = u.shape
    f32 = jnp.float32
    u32 = u.astype(f32).reshape(bsz, seq_len, SSM_GROUPS, SSM_GROUP)
    a_re = a_re.astype(f32)
    a_im = a_im.astype(f32)
    dt = jnp.exp(log_dt.astype(f32))[:, None]
    mag = jnp.exp(dt * a_re)
    abar_re = mag * jnp.cos(dt * a_im)
    abar_im = mag * jnp.sin(dt * a_im)
    den = a_re * a_re + a_im * a_im
    p_re = abar_re - 1.0
    f_re = (p_re * a_re + abar_im * a_im) / den
    f_im = (abar_im * a_re - p_re * a_im) / den
    b_re = b_re.astype(f32)
    b_im = b_im.astype(f32)
    bbar_re = f_re[..., None] * b_re - f_im[..., None] * b_im
    bbar_im = f_re[..., None] * b_im + f_im[..., None] * b_re
    bu_re = jnp.einsum('blgp,gnp->blgn', u32, bbar_re)
    bu_im = jnp.einsum('blgp,gnp->blgn', u32, bbar_im)
    a_seq_re = jnp.broadcast_to(abar_re, bu_re.shape)
    a_seq_im = jnp.broadcast_to(abar_im, bu_im.shape)
    _, _, s_re, s_im = lax.associative_scan(
        _ssm_combine, (a_seq_re, a_seq_im, bu_re, bu_im), axis=1)
    y = (jnp.einsum('blgn,gpn->blgp', s_re, c_re.astype(f32))
         - jnp.einsum('blgn,gpn->blgp', s_im, c_im.astype(f32)))
    y = y.reshape(bsz, seq_len, SSM_WIDTH) + d_skip.astype(f32) * u32.reshape(bsz, seq_len, SSM_WIDTH)
    y = jax.nn.gelu(y).astype(u.dtype)
    return y * jax.nn.sigmoid(y @ w_glu + b_glu)

def t5_bucket(rel):
    n = jnp.maximum(rel, 0)
    max_exact = REL_BUCKETS // 2
    nf = jnp.maximum(n, 1).astype(jnp.float32)
    large = max_exact + (jnp.log(nf / max_exact) / math.log(REL_MAX_DIST / max_exact)
                         * (REL_BUCKETS - max_exact)).astype(jnp.int32)
    large = jnp.minimum(large, REL_BUCKETS - 1)
    return jnp.where(n < max_exact, n, large)

def moba_attention(q, k, v, rel_bias):
    bsz, seq_len = q.shape[0], q.shape[1]
    n_blk = -(-seq_len // MOBA_BLOCK)
    pad = n_blk * MOBA_BLOCK - seq_len
    n_sel = min(MOBA_TOPK, n_blk - 1)
    q = q.transpose(0, 2, 1, 3)
    k = jnp.pad(k.transpose(0, 2, 1, 3), ((0, 0), (0, 0), (0, pad), (0, 0)))
    v = jnp.pad(v.transpose(0, 2, 1, 3), ((0, 0), (0, 0), (0, pad), (0, 0)))
    kb = k.reshape(bsz, ATTN_HEADS, n_blk, MOBA_BLOCK, HEAD_DIM)
    vb = v.reshape(bsz, ATTN_HEADS, n_blk, MOBA_BLOCK, HEAD_DIM)
    kmean = jnp.mean(kb.astype(jnp.float32), axis=3).astype(k.dtype)
    bias_table = rel_bias.T
    head_ix = jnp.arange(ATTN_HEADS)
    n_qblk = seq_len // Q_BLOCK
    scale = HEAD_DIM ** -0.5
    blk_off = jnp.arange(MOBA_BLOCK)

    def one_block(i):
        b = i // n_qblk
        q0 = (i % n_qblk) * Q_BLOCK
        own = q0 // MOBA_BLOCK
        qc = lax.dynamic_slice_in_dim(lax.dynamic_index_in_dim(q, b, 0, keepdims=False),
                                      q0, Q_BLOCK, axis=1)
        kb_b = lax.dynamic_index_in_dim(kb, b, 0, keepdims=False)
        vb_b = lax.dynamic_index_in_dim(vb, b, 0, keepdims=False)
        q_pos = q0 + jnp.arange(Q_BLOCK)
        k_own = lax.dynamic_index_in_dim(kb_b, own, 1, keepdims=False)
        v_own = lax.dynamic_index_in_dim(vb_b, own, 1, keepdims=False)
        rel_own = q_pos[:, None] - (own * MOBA_BLOCK + blk_off)[None, :]
        s_own = (jnp.einsum('hqd,hsd->hqs', qc, k_own).astype(jnp.float32) * scale
                 + bias_table[:, t5_bucket(rel_own)].astype(jnp.float32))
        s_own = jnp.where(rel_own[None] >= 0, s_own, NEG_INF)
        if n_sel == 0:
            p = jax.nn.softmax(s_own, axis=-1).astype(v.dtype)
            return jnp.einsum('hqs,hsd->hqd', p, v_own)
        gate = jnp.einsum('hqd,hnd->hqn', qc, kmean[b]).astype(jnp.float32)
        gate = jnp.where(jnp.arange(n_blk) < own, gate, NEG_INF)
        _, sel = lax.top_k(gate, n_sel)
        valid = jnp.arange(n_sel) < own
        kg = kb_b[head_ix[:, None, None], sel]
        vg = vb_b[head_ix[:, None, None], sel]
        rel_sel = q_pos[None, :, None, None] - (sel[..., None] * MOBA_BLOCK + blk_off)
        s_sel = (jnp.einsum('hqd,hqksd->hqks', qc, kg).astype(jnp.float32) * scale
                 + bias_table[head_ix[:, None, None, None], t5_bucket(rel_sel)].astype(jnp.float32))
        s_sel = jnp.where(valid[None, None, :, None], s_sel, NEG_INF)
        s = jnp.concatenate([s_sel.reshape(ATTN_HEADS, Q_BLOCK, n_sel * MOBA_BLOCK), s_own], axis=-1)
        p = jax.nn.softmax(s, axis=-1).astype(v.dtype)
        p_sel = p[..., :n_sel * MOBA_BLOCK].reshape(ATTN_HEADS, Q_BLOCK, n_sel, MOBA_BLOCK)
        return (jnp.einsum('hqks,hqksd->hqd', p_sel, vg)
                + jnp.einsum('hqs,hsd->hqd', p[..., n_sel * MOBA_BLOCK:], v_own))

    o = lax.map(one_block, jnp.arange(bsz * n_qblk))
    o = o.reshape(bsz, n_qblk, ATTN_HEADS, Q_BLOCK, HEAD_DIM).transpose(0, 1, 3, 2, 4)
    return o.reshape(bsz, seq_len, ATTN_WIDTH)

def first_inputs(seed: int = 0) -> dict:
    key = jax.random.key(seed)
    ks = jax.random.split(key, 24)
    f32 = jnp.float32
    nrm = lambda k, shape, s: jax.random.normal(k, shape, f32) * s
    n_idx = jnp.arange(SSM_STATE, dtype=f32)
    a_re = -0.5 + nrm(ks[4], (DEPTH, SSM_GROUPS, SSM_STATE), 0.01)
    a_im = math.pi * n_idx + nrm(ks[5], (DEPTH, SSM_GROUPS, SSM_STATE), 0.01)
    log_dt = jax.random.uniform(ks[6], (DEPTH, SSM_GROUPS), f32,
                                math.log(DT_MIN), math.log(DT_MAX))
    return {
        "x": nrm(ks[0], (BATCH, SEQ, D_MODEL), 1.0),
        "c": nrm(ks[1], (BATCH, D_MODEL), 1.0),
        "rel_bias": nrm(ks[2], (REL_BUCKETS, ATTN_HEADS), 0.5),
        "w_ada": nrm(ks[3], (DEPTH, D_MODEL, N_MOD * D_MODEL), 0.5 * D_MODEL ** -0.5),
        "b_ada": nrm(ks[7], (DEPTH, N_MOD * D_MODEL), 0.02),
        "norm_mix_g": 1.0 + nrm(ks[8], (DEPTH, D_MODEL), 0.02),
        "w_in": nrm(ks[9], (DEPTH, D_MODEL, IN_WIDTH), D_MODEL ** -0.5),
        "ssm_a_re": a_re,
        "ssm_a_im": a_im,
        "ssm_log_dt": log_dt,
        "ssm_b_re": nrm(ks[10], (DEPTH, SSM_GROUPS, SSM_STATE, SSM_GROUP), (2 * SSM_GROUP) ** -0.5),
        "ssm_b_im": nrm(ks[11], (DEPTH, SSM_GROUPS, SSM_STATE, SSM_GROUP), (2 * SSM_GROUP) ** -0.5),
        "ssm_c_re": nrm(ks[12], (DEPTH, SSM_GROUPS, SSM_GROUP, SSM_STATE), (2 * SSM_STATE) ** -0.5),
        "ssm_c_im": nrm(ks[13], (DEPTH, SSM_GROUPS, SSM_GROUP, SSM_STATE), (2 * SSM_STATE) ** -0.5),
        "ssm_d": nrm(ks[14], (DEPTH, SSM_WIDTH), 1.0),
        "w_glu": nrm(ks[15], (DEPTH, SSM_WIDTH, SSM_WIDTH), SSM_WIDTH ** -0.5),
        "b_glu": nrm(ks[16], (DEPTH, SSM_WIDTH), 0.02),
        "w_proj_ssm": nrm(ks[17], (DEPTH, SSM_WIDTH, D_MODEL), SSM_WIDTH ** -0.5),
        "w_proj_attn": nrm(ks[18], (DEPTH, ATTN_WIDTH, D_MODEL), ATTN_WIDTH ** -0.5),
        "w_out": nrm(ks[19], (DEPTH, D_MODEL, D_MODEL), D_MODEL ** -0.5),
        "norm_mlp_g": 1.0 + nrm(ks[20], (DEPTH, D_MODEL), 0.02),
        "w_ff1": nrm(ks[21], (DEPTH, D_MODEL, D_FF), D_MODEL ** -0.5),
        "w_ff2": nrm(ks[22], (DEPTH, D_FF, D_MODEL), D_FF ** -0.5),
        "norm_final_g": 1.0 + nrm(ks[23], (D_MODEL,), 0.02),
    }

def first_block(x, c, rel_bias, w_ada, b_ada, norm_mix_g, w_in, ssm_a_re, ssm_a_im, ssm_log_dt,
              ssm_b_re, ssm_b_im, ssm_c_re, ssm_c_im, ssm_d, w_glu, b_glu, w_proj_ssm,
              w_proj_attn, w_out, norm_mlp_g, w_ff1, w_ff2, norm_final_g):
    bsz, seq_len, _ = x.shape
    split_at = [SSM_WIDTH, SSM_WIDTH + ATTN_WIDTH, SSM_WIDTH + 2 * ATTN_WIDTH,
                SSM_WIDTH + 3 * ATTN_WIDTH, SSM_WIDTH + 3 * ATTN_WIDTH + D_MODEL]
    c_act = jax.nn.silu(c)
    for l in range(DEPTH):
        mod = c_act @ w_ada[l] + b_ada[l]
        sh1, sc1, g1, sh2, sc2, g2 = [m[:, None, :] for m in jnp.split(mod, N_MOD, axis=-1)]
        h = rms_norm(x, norm_mix_g[l]) * (1.0 + sc1) + sh1
        proj = h @ w_in[l]
        u, q, k, v, ga, gb = jnp.split(proj, split_at, axis=-1)
        y_ssm = s5_branch(u, ssm_a_re[l], ssm_a_im[l], ssm_log_dt[l], ssm_b_re[l], ssm_b_im[l],
                          ssm_c_re[l], ssm_c_im[l], ssm_d[l], w_glu[l], b_glu[l])
        shp = (bsz, seq_len, ATTN_HEADS, HEAD_DIM)
        y_att = moba_attention(q.reshape(shp), k.reshape(shp), v.reshape(shp), rel_bias)
        merged = (jax.nn.sigmoid(ga) * (y_ssm @ w_proj_ssm[l])
                  + jax.nn.sigmoid(gb) * (y_att @ w_proj_attn[l]))
        x = x + g1 * (merged @ w_out[l])
        h2 = rms_norm(x, norm_mlp_g[l]) * (1.0 + sc2) + sh2
        x = x + g2 * (jnp.square(jax.nn.relu(h2 @ w_ff1[l])) @ w_ff2[l])
    return rms_norm(x, norm_final_g)


D_RNN = 2048
N_RNN_BLOCKS = 8
RNN_BLOCK = D_RNN // N_RNN_BLOCKS
CONV_WIDTH = 4
LRU_C = 8.0
N_Q_HEADS = 32
N_KV_HEADS = 4
HEAD_DIM_2 = 64
Q_GROUP = N_Q_HEADS // N_KV_HEADS
WINDOW = 128
ATTN_BLOCK = 128
ROPE_THETA = 10000.0
D_FF_2 = 4 * D_MODEL
RMS_EPS = 1e-6
NEG_INF_2 = -1e30

IN_SPLITS = (D_RNN, D_RNN, N_Q_HEADS * HEAD_DIM_2, N_KV_HEADS * HEAD_DIM_2, N_KV_HEADS * HEAD_DIM_2, D_MODEL, D_MODEL)
IN_OFFSETS = tuple(int(o) for o in np.cumsum(IN_SPLITS)[:-1])
D_IN = int(sum(IN_SPLITS))


def rmsnorm(x, g):
    xf = x.astype(jnp.float32)
    y = xf * lax.rsqrt(jnp.mean(xf * xf, axis=-1, keepdims=True) + RMS_EPS)
    return (y * g.astype(jnp.float32)).astype(x.dtype)

def rope(x, positions):
    half = HEAD_DIM_2 // 2
    inv_freq = ROPE_THETA ** (-jnp.arange(0, HEAD_DIM_2, 2, dtype=jnp.float32) / HEAD_DIM_2)
    ang = positions.astype(jnp.float32)[..., None] * inv_freq
    cos = jnp.cos(ang)[:, :, None, :]
    sin = jnp.sin(ang)[:, :, None, :]
    xf = x.astype(jnp.float32)
    x1, x2 = xf[..., :half], xf[..., half:]
    out = jnp.concatenate([x1 * cos - x2 * sin, x2 * cos + x1 * sin], axis=-1)
    return out.astype(x.dtype)

def causal_depthwise_conv(x, w, b):
    S = x.shape[1]
    xp = jnp.pad(x, ((0, 0), (CONV_WIDTH - 1, 0), (0, 0)))
    y = b
    for k in range(CONV_WIDTH):
        y = y + xp[:, k:k + S] * w[k]
    return y

def rg_lru(x, positions, w_a, b_a, w_x, b_x, lam):
    B, S, _ = x.shape
    xf = x.astype(jnp.float32)
    xb = xf.reshape(B, S, N_RNN_BLOCKS, RNN_BLOCK)
    r = jax.nn.sigmoid(jnp.einsum('bsni,nij->bsnj', xb, w_a.astype(jnp.float32)).reshape(B, S, D_RNN) + b_a)
    i = jax.nn.sigmoid(jnp.einsum('bsni,nij->bsnj', xb, w_x.astype(jnp.float32)).reshape(B, S, D_RNN) + b_x)
    log_a = -LRU_C * r * jax.nn.softplus(-lam.astype(jnp.float32))
    a = jnp.exp(log_a)
    mult = jnp.sqrt(-jnp.expm1(2.0 * log_a))
    reset = (positions == 0)[..., None]
    a = jnp.where(reset, 0.0, a)
    mult = jnp.where(reset, 1.0, mult)
    b = mult * (i * xf)

    def combine(left, right):
        a_l, b_l = left
        a_r, b_r = right
        return a_l * a_r, a_r * b_l + b_r

    _, h = lax.associative_scan(combine, (a, b), axis=1)
    return h.astype(x.dtype)

def sliding_window_sink_attention(q, k, v, sinks):
    B, S = q.shape[0], q.shape[1]
    T = ATTN_BLOCK
    NB = S // T
    scale = HEAD_DIM_2 ** -0.5
    qb = q.reshape(B, NB, T, N_KV_HEADS, Q_GROUP, HEAD_DIM_2) * scale
    kb = k.reshape(B, NB, T, N_KV_HEADS, HEAD_DIM_2)
    vb = v.reshape(B, NB, T, N_KV_HEADS, HEAD_DIM_2)
    pad = ((0, 0), (1, 0), (0, 0), (0, 0), (0, 0))
    kk = jnp.concatenate([jnp.pad(kb, pad)[:, :-1], kb], axis=2)
    vv = jnp.concatenate([jnp.pad(vb, pad)[:, :-1], vb], axis=2)
    scores = jnp.einsum('bnqhgd,bnkhd->bnhgqk', qb, kk).astype(jnp.float32)
    qi = jnp.arange(T)[:, None]
    ki = jnp.arange(2 * T)[None, :]
    dist = qi + T - ki
    band = (dist >= 0) & (dist < WINDOW)
    not_pad = (jnp.arange(NB)[:, None, None] > 0) | (ki >= T)[None]
    valid = (band[None] & not_pad)[None, :, None, None]
    scores = jnp.where(valid, scores, NEG_INF_2)
    sink = sinks.astype(jnp.float32).reshape(N_KV_HEADS, Q_GROUP)[None, None, :, :, None, None]
    m = jnp.maximum(jnp.max(scores, axis=-1, keepdims=True), sink)
    p = jnp.exp(scores - m)
    denom = jnp.sum(p, axis=-1, keepdims=True) + jnp.exp(sink - m)
    probs = (p / denom).astype(v.dtype)
    out = jnp.einsum('bnhgqk,bnkhd->bnqhgd', probs, vv)
    return out.reshape(B, S, N_Q_HEADS * HEAD_DIM_2)

def second_inputs(seed: int = 0) -> dict:
    key = jax.random.key(seed)
    ks = jax.random.split(key, 20)
    f32 = jnp.float32
    L = DEPTH

    def nrm(k, shape, scale):
        return jax.random.normal(k, shape, f32) * scale

    def gain(k):
        return 1.0 + 0.05 * jax.random.normal(k, (L, D_MODEL), f32)

    x = jax.random.normal(ks[0], (BATCH, SEQ, D_MODEL), f32)
    positions = jnp.broadcast_to(jnp.arange(SEQ, dtype=jnp.int32)[None, :], (BATCH, SEQ))
    u = jax.random.uniform(ks[9], (L, D_RNN), f32, 0.9, 0.999)
    a0 = u ** (1.0 / LRU_C)
    lru_lambda = jnp.log(a0) - jnp.log1p(-a0)
    return {
        "x": x,
        "positions": positions,
        "norm_mix_pre": gain(ks[1]),
        "w_in": nrm(ks[2], (L, D_MODEL, D_IN), D_MODEL ** -0.5),
        "conv_w": nrm(ks[3], (L, CONV_WIDTH, D_RNN), CONV_WIDTH ** -0.5),
        "conv_b": nrm(ks[4], (L, D_RNN), 0.01),
        "w_rg_a": nrm(ks[5], (L, N_RNN_BLOCKS, RNN_BLOCK, RNN_BLOCK), RNN_BLOCK ** -0.5),
        "b_rg_a": nrm(ks[6], (L, D_RNN), 0.01),
        "w_rg_x": nrm(ks[7], (L, N_RNN_BLOCKS, RNN_BLOCK, RNN_BLOCK), RNN_BLOCK ** -0.5),
        "b_rg_x": nrm(ks[8], (L, D_RNN), 0.01),
        "lru_lambda": lru_lambda,
        "attn_sinks": nrm(ks[10], (L, N_Q_HEADS), 0.5),
        "w_rnn_proj": nrm(ks[11], (L, D_RNN, D_MODEL), D_RNN ** -0.5),
        "w_attn_proj": nrm(ks[12], (L, N_Q_HEADS * HEAD_DIM_2, D_MODEL), (N_Q_HEADS * HEAD_DIM_2) ** -0.5),
        "w_out": nrm(ks[13], (L, D_MODEL, D_MODEL), D_MODEL ** -0.5),
        "norm_mix_post": gain(ks[14]),
        "norm_mlp_pre": gain(ks[15]),
        "w_mlp_up": nrm(ks[16], (L, D_MODEL, D_FF_2), D_MODEL ** -0.5),
        "w_mlp_down": nrm(ks[17], (L, D_FF_2, D_MODEL), D_FF_2 ** -0.5),
        "norm_mlp_post": gain(ks[18]),
    }

def second_block(x, positions, norm_mix_pre, w_in, conv_w, conv_b, w_rg_a, b_rg_a, w_rg_x, b_rg_x, lru_lambda, attn_sinks, w_rnn_proj, w_attn_proj, w_out, norm_mix_post, norm_mlp_pre, w_mlp_up, w_mlp_down, norm_mlp_post):
    B, S, _ = x.shape
    for l in range(DEPTH):
        h = rmsnorm(x, norm_mix_pre[l])
        proj = h @ w_in[l]
        xr, yr, q, k, v, g_rnn, g_attn = jnp.split(proj, IN_OFFSETS, axis=-1)
        xr = causal_depthwise_conv(xr, conv_w[l], conv_b[l])
        xr = rg_lru(xr, positions, w_rg_a[l], b_rg_a[l], w_rg_x[l], b_rg_x[l], lru_lambda[l])
        y_rnn = xr * jax.nn.gelu(yr)
        q = rope(q.reshape(B, S, N_Q_HEADS, HEAD_DIM_2), positions)
        k = rope(k.reshape(B, S, N_KV_HEADS, HEAD_DIM_2), positions)
        v = v.reshape(B, S, N_KV_HEADS, HEAD_DIM_2)
        y_att = sliding_window_sink_attention(q, k, v, attn_sinks[l])
        mix = jax.nn.sigmoid(g_rnn) * (y_rnn @ w_rnn_proj[l]) + jax.nn.sigmoid(g_attn) * (y_att @ w_attn_proj[l])
        x = x + rmsnorm(mix @ w_out[l], norm_mix_post[l])
        h = rmsnorm(x, norm_mlp_pre[l])
        u = jnp.square(jax.nn.relu(h @ w_mlp_up[l]))
        x = x + rmsnorm(u @ w_mlp_down[l], norm_mlp_post[l])
    return x


def setup_inputs(seed=0):
    out = dict(first_inputs(seed))
    for name, value in second_inputs(seed + 1).items():
        if name != "x":
            out[name + "_2"] = value
    return out


def reference(
    x, c, rel_bias, w_ada, b_ada, norm_mix_g, w_in, ssm_a_re, ssm_a_im, ssm_log_dt, ssm_b_re,
    ssm_b_im, ssm_c_re, ssm_c_im, ssm_d, w_glu, b_glu, w_proj_ssm, w_proj_attn, w_out,
    norm_mlp_g, w_ff1, w_ff2, norm_final_g, positions_2, norm_mix_pre_2, w_in_2, conv_w_2,
    conv_b_2, w_rg_a_2, b_rg_a_2, w_rg_x_2, b_rg_x_2, lru_lambda_2, attn_sinks_2, w_rnn_proj_2,
    w_attn_proj_2, w_out_2, norm_mix_post_2, norm_mlp_pre_2, w_mlp_up_2, w_mlp_down_2,
    norm_mlp_post_2,
):
    x = first_block(
        x, c, rel_bias, w_ada, b_ada, norm_mix_g, w_in, ssm_a_re, ssm_a_im, ssm_log_dt,
        ssm_b_re, ssm_b_im, ssm_c_re, ssm_c_im, ssm_d, w_glu, b_glu, w_proj_ssm, w_proj_attn,
        w_out, norm_mlp_g, w_ff1, w_ff2, norm_final_g,
    )
    return second_block(
        x, positions_2, norm_mix_pre_2, w_in_2, conv_w_2, conv_b_2, w_rg_a_2, b_rg_a_2,
        w_rg_x_2, b_rg_x_2, lru_lambda_2, attn_sinks_2, w_rnn_proj_2, w_attn_proj_2, w_out_2,
        norm_mix_post_2, norm_mlp_pre_2, w_mlp_up_2, w_mlp_down_2, norm_mlp_post_2,
    )


_drawn_inputs = setup_inputs


def setup_inputs(seed=0):
    import zlib

    import numpy as np

    out = dict(_drawn_inputs(seed))
    spreads = {}
    factors = {'rel_bias': 2.681,
     'norm_mix_g': 8.0,
     'ssm_a_re': 64.0,
     'ssm_a_im': 64.0,
     'ssm_log_dt': 64.0,
     'ssm_b_re': 64.0,
     'ssm_b_im': 64.0,
     'ssm_c_re': 64.0,
     'ssm_c_im': 64.0,
     'b_glu': 35.349,
     'norm_mlp_g': 5.078,
     'b_rg_a_2': 61.472,
     'b_rg_x_2': 8.0,
     'attn_sinks_2': 4.004,
     'conv_b_2': 3.519}
    for name, (base, spread) in spreads.items():
        noise = np.random.default_rng([zlib.crc32(name.encode()), seed]).standard_normal(out[name].shape)
        drawn = base * np.exp(spread * noise) if base else spread * noise
        out[name] = __import__('jax').numpy.asarray(drawn.astype(out[name].dtype))
    for name, factor in factors.items():
        out[name] = (out[name] * factor).astype(out[name].dtype)
    return out
```

```python
from contextlib import ExitStack
import math

import numpy as np
import concourse.bass as bass
from concourse import mybir
from concourse.alu_op_type import AluOpType as ALU

F32 = mybir.dt.float32
F32R = mybir.dt.float32r
I32 = mybir.dt.int32
ACT = mybir.ActivationFunctionType
AX = mybir.AxisListType.X

P = 128
T = 256
D = 2048
NEG = -1e30
RAWN = 5
SPN = 3
LOOK = 2
MAGIC = 12582912.0
TWO_PI = 2.0 * math.pi
GELU_C = 0.7978845608028654
GELU_A = 0.044715


def two_pi_parts():
    c1 = np.float32(6.28125)
    c2 = np.float32(np.round((TWO_PI - float(c1)) * 2.0 ** 21) / 2.0 ** 21)
    c3 = np.float32(TWO_PI - float(c1) - float(c2))
    return float(c1), float(c2), float(c3)


def bucket_of(n):
    if n < 16:
        return n
    v = np.log(np.float32(n) / np.float32(16)) / np.float32(math.log(128 / 16)) * np.float32(16)
    return min(16 + int(np.float32(v)), 31)


def constants():
    ident = np.eye(P, dtype=np.float32)
    hot = np.zeros((32, 384), np.float32)
    neg = np.zeros((8, 384), np.float32)
    for j in range(384):
        rel = 255 - j
        if rel >= 0:
            hot[bucket_of(rel), j] = 1.0
        else:
            neg[:, j] = NEG
    inv = np.float32(10000.0) ** (-np.arange(0, 64, 2, dtype=np.float32) / np.float32(64))
    part = np.zeros((P, 4), np.float32)
    part[:, 0] = np.tile(inv.astype(np.float32), 4)
    par = (np.arange(P) // 16) % 2
    part[:, 1] = (par == 0)
    part[:, 2] = (par == 1)
    swap = np.zeros((P, P), np.float32)
    for m in range(P):
        b, r = m // 64 * 64, m % 64
        if r < 32:
            swap[b + r + 32, m] = -1.0
        else:
            swap[b + r - 32, m] = 1.0
    q, k = np.arange(P)[:, None], np.arange(P)[None, :]
    mask = np.concatenate([np.where(k > q, 0.0, NEG), np.where(k <= q, 0.0, NEG)], 1).astype(np.float32)
    swap = np.concatenate([swap, ident[::-1]], 1)
    return {"c_ident": ident, "c_hot": hot, "c_neg": neg, "c_part": part, "c_swap": swap, "c_mask": mask}


class Engine:

    def __init__(self, e, sem):
        self.e, self.sem, self.n, self.seen = e, sem, 0, {}

    def wait(self, *tokens):
        for t in tokens:
            if t is None:
                continue
            if isinstance(t, list):
                self.wait(*t)
                continue
            sem, v = t
            if self.seen.get(id(sem), 0) < v:
                self.seen[id(sem)] = v
                self.e.wait_ge(sem, v)

    def do(self, f, *tokens):
        self.wait(*tokens)
        self.n += 1
        f(self.e).then_inc(self.sem, 1)
        return (self.sem, self.n)

    def quiet(self, f, *tokens):
        self.wait(*tokens)
        f(self.e)


def build(nc, I, out, scr_x, scr_b):
    with ExitStack() as ctx:
        _build(nc, ctx, I, out, scr_x, scr_b)


def _build(nc, ctx, I, out, scr_x, scr_b):
    def sb(name, shape, dt=F32):
        return ctx.enter_context(nc.sbuf_tensor(name, shape, dt))

    def sem(name):
        return ctx.enter_context(nc.semaphore(name))

    raw = sb("raw", [P, RAWN, 1024])
    whi = sb("whi", [P, SPN, 1024], F32R)
    wlo = sb("wlo", [P, SPN, 1024], F32R)
    R = sb("R", [P, 16384], F32R)
    F = sb("F", [P, 21504])
    ident = sb("ident", [P, P])
    ones = sb("ones", [P, P])
    cols = sb("cols", [P, 480])
    mod = sb("mod", [P, 96])
    der = sb("der", [P, 16, 16])
    PS = ctx.enter_context(nc.psum_tensor("PS", [P, 8, 512], F32))

    pe = Engine(nc.tensor, sem("s_pe"))
    act = Engine(nc.scalar, sem("s_act"))
    dve = Engine(nc.vector, sem("s_dve"))
    pool = Engine(nc.gpsimd, sem("s_pool"))
    sp = Engine(nc.sync, sem("s_sp"))
    raw_sem = [sem(f"s_raw{i}") for i in range(RAWN)]
    nsem = [0]

    def dma(eng, pairs, *tokens):
        s = sem(f"s_dma{nsem[0]}")
        nsem[0] += 1
        eng.wait(*tokens)
        for o, i in pairs:
            eng.e.dma_start(o, i).then_inc(s, 16)
        return (s, 16 * len(pairs))

    def fv(off, n):
        return F[:, off:off + n]

    def f3(off, k, n=T):
        return F[:, off:off + k * n].rearrange("p (k n) -> p k n", k=k)

    class Operand:

        def __init__(self, *blocks):
            self.b = blocks
            self.ready = [None] * (8 * len(blocks))

        def hi(self, k, n=1):
            o = self.b[k // 8] * 4096 + (k % 8) * T
            return R[:, o:o + n * T]

        def lo(self, k, n=1):
            o = self.b[k // 8] * 4096 + 2048 + (k % 8) * T
            return R[:, o:o + n * T]

    def split_out(op, k, n, src, scale, *tokens):
        a = act.do(lambda e: e.activation(op.hi(k, n), src, ACT.Copy, scale=scale), *tokens)
        if scale == 1.0:
            b = dve.do(lambda e: e.tensor_tensor(op.lo(k, n), src, op.hi(k, n).bitcast(F32), ALU.subtract), a)
        else:
            b = dve.do(lambda e: e.scalar_tensor_tensor(op.lo(k, n), src, scale, op.hi(k, n).bitcast(F32),
                                                        ALU.mult, ALU.subtract), a)
        for j in range(k, k + n):
            op.ready[j] = b
        return b

    units = []
    state = {"prep": 0, "w": 0, "sent": 0}
    released = {}
    used = {}

    def send(j):
        u = units[j]
        s = j % RAWN
        toks = released[j - RAWN] if j >= RAWN else []
        sp.wait(*toks)
        dst = raw[:, s, :].rearrange("p (k n) -> p k n", k=u["nk"])
        src = u["src"]
        sp.e.dma_start(dst, src).then_inc(raw_sem[s], 16)

    def landed(j):
        return (raw_sem[j % RAWN], 16 * (j // RAWN + 1))

    def prep(j):
        u = units[j]
        r = raw[:, j % RAWN, :]
        if u["kind"] == "w":
            w = state["w"]
            state["w"] += 1
            u["w"] = w
            s = w % SPN
            free = used.get(w - SPN)
            a = act.do(lambda e: e.activation(whi[:, s, :], r, ACT.Copy), landed(j), free)
            b = dve.do(lambda e: e.tensor_tensor(wlo[:, s, :], r, whi[:, s, :].bitcast(F32), ALU.subtract),
                       landed(j), a, free)
            u["ready"] = [a, b]
            released[j] = [a, b]
        else:
            released[j] = [u["use"](r, landed(j))]
            if u.get("close"):
                ada_close(*u["close"])
        if j + RAWN < len(units):
            send(j + RAWN)

    def advance(to):
        to = min(to, len(units) - 1)
        while state["prep"] <= to:
            prep(state["prep"])
            state["prep"] += 1

    gbuf = [0]
    gfree = [None, None]

    class Panel:
        pass

    panels = []

    def add_panel(srcs, nk, mms, operand, evac, before=None, bg=1):
        p = Panel()
        p.units = []
        for s in srcs:
            u = {"kind": "w", "src": s, "nk": nk}
            p.units.append(u)
            units.append(u)
        p.mms, p.operand, p.evac, p.before, p.bg = mms, operand, evac, before, bg
        panels.append(p)
        return p

    def add_ada(src, use):
        units.append({"kind": "ada", "src": src, "nk": 1, "use": use})

    background = []
    side = []

    def step(queue=None):
        q = background if queue is None else queue
        while q:
            try:
                next(q[0])
                return
            except StopIteration:
                q.pop(0)

    def finish_bg(g):
        while g in background:
            step()

    index_of = {}

    def run_panel(p):
        if p.before:
            p.before()
        b = gbuf[0] % 2
        gbuf[0] += 1
        pe.wait(gfree[b])
        seen_bank = set()
        last = len(p.units) - 1
        for n, u in enumerate(p.units):
            j = index_of[id(u)]
            advance(j)
            pe.wait(*u["ready"])
            s = u["w"] % SPN
            todo = p.mms(n)
            for col, k, m in todo:
                pe.wait(p.operand.ready[k])
                o = PS[:, 2 * b + m // 2, (m % 2) * T:(m % 2) * T + T]
                bank = m // 2
                for a, (w, x) in enumerate(((whi, p.operand.hi(k)), (whi, p.operand.lo(k)), (wlo, p.operand.hi(k)))):
                    first = bank not in seen_bank
                    seen_bank.add(bank)
                    stop = n == last and a == 2 and (col, k, m) == [t for t in todo if t[2] == m][-1]
                    fn = lambda e, o=o, w=w, x=x, first=first, stop=stop, col=col, s=s: e.matmul(
                        o, w[:, s, col:col + P], x, start=first, stop=stop, skip_group_check=True)
                    if a == 2 and (col, k, m) == todo[-1]:
                        tok = pe.do(fn)
                    else:
                        pe.quiet(fn)
            used[u["w"]] = tok
            advance(j + LOOK)
            if n < last:
                for _ in range(p.bg):
                    step()
                step(side)
        full = PS[:, 2 * b:2 * b + 2, :].rearrange("p a n -> p (a n)")
        gfree[b] = p.evac(full, tok)
        for _ in range(p.bg):
            step()
        step(side)

    def std(W, k0, nkt, c0):
        v = W.rearrange("(k p) n -> p k n", p=P)
        srcs = [v[:, k0 + 2 * u:k0 + 2 * u + 2, c0:c0 + 512] for u in range(nkt // 2)]
        mms = lambda u: [(kk * 512 + m * P, 2 * u + kk, m) for kk in range(2) for m in range(4)]
        return srcs, mms

    GA, GB = 0, 4096
    U = 8192
    E0 = 10240
    SW = 14336
    LB = 17408
    CT = 19456
    XN = 0
    Q, K, V = 10240, 12288, 14336
    BH = 16384
    AW = 18432
    X = 0
    STG = 8192
    w2 = lambda n: I[n].rearrange("o a b -> (o a) b")
    rows = lambda n: I[n].rearrange("o (k p) -> (o k) p", p=P)
    S0, S1, S2, S3 = (fv(STG + 128 * i, 128) for i in range(4))
    small = [
        (ident[:, :], I["c_ident"]),
        (S0[0:16, :], rows("c")), (S0[16:32, :], rows("norm_mix_g")), (S0[32:128, :], rows("b_ada")),
        (S1[0:16, :], rows("norm_mlp_g")), (S1[16:32, :], I["norm_final_g"].rearrange("(k p) -> k p", p=P)),
        (S1[32:40, :], rows("ssm_d")), (S1[40:48, :], rows("b_glu")),
        (S1[48:64, :], rows("norm_mix_pre_2")), (S1[64:80, :], rows("norm_mix_post_2")),
        (S1[80:96, :], rows("norm_mlp_pre_2")), (S1[96:112, :], rows("norm_mlp_post_2")),
        (S1[112:128, :], rows("lru_lambda_2")),
        (S2[0:64, :], I["conv_w_2"].rearrange("o w (k p) -> (o w k) p", p=P)),
        (S2[64:80, :], rows("conv_b_2")), (S2[80:96, :], rows("b_rg_a_2")), (S2[96:112, :], rows("b_rg_x_2")),
        (S3[0:32, :], I["ssm_a_re"].rearrange("o (t s) n -> (o t) (s n)", s=2)),
        (S3[32:64, :], I["ssm_a_im"].rearrange("o (t s) n -> (o t) (s n)", s=2)),
    ]
    ldt = fv(STG + 512, 2)
    small.append((ldt[64:96, :], I["ssm_log_dt"].rearrange("o (t s) -> (o t) s", s=2)))
    t_small = dma(act, small)
    xn = f3(XN, 2, D)
    t_x = dma(act, [(xn[:, i, :], I["x"][0, i * P:(i + 1) * P, :]) for i in range(2)])
    relb = fv(STG + 516, 8)
    hot = fv(STG + 524, 384)
    negr = fv(STG + 908, 384)
    part = sb("part", [P, 4])
    t_hot = dma(act, [(relb[0:32, :], I["rel_bias"]), (hot[0:32, :], I["c_hot"]), (negr[0:8, :], I["c_neg"]),
                      (part[:, :], I["c_part"])])
    BB = 9600 + 4096
    bsr = f3(BB, 2, 512)
    csr = f3(BB + 1024, 2, 512)
    gn = "o (t s) n p -> (s n) (o t) p"
    t_bc = dma(act, [
        (bsr[:, 0, :].rearrange("q (t p) -> q t p", t=32), I["ssm_b_re"].rearrange("o (t s) n p -> (o s n) t p", s=2)),
        (bsr[:, 1, :].rearrange("q (t p) -> q t p", t=32), I["ssm_b_im"].rearrange("o (t s) n p -> (o s n) t p", s=2)),
        (csr[:, 0, :].rearrange("q (f n) -> q f n", f=8), I["ssm_c_re"].rearrange("o (f g) p n -> (o g p) f n", g=8)),
        (csr[:, 1, :].rearrange("q (f n) -> q f n", f=8), I["ssm_c_im"].rearrange("o (f g) p n -> (o g p) f n", g=8)),
    ])
    C_C, C_G1, C_BADA = 0, 16, 32
    C_GM, C_GF, C_SD, C_BG = 128, 144, 160, 168
    C_PRE, C_POST, C_MPRE, C_MPOST, C_LAM = 176, 192, 208, 224, 240
    C_CW, C_CB, C_BA, C_BX = 256, 320, 336, 352
    C_AR, C_AI, C_LD = 384, 416, 448

    dcol = lambda i, n=16: der[:, i, 0:n]
    cact, A1, A2, hbg, spc, hba, hbx, eps = (dcol(i) for i in range(8))

    t_one = dve.do(lambda e: e.memset(ones[:, :], 1.0))
    t_eps = dve.do(lambda e: e.memset(eps, 1e-6))
    t = dve.do(lambda e: e.tensor_copy(S3[64:96, :].rearrange("p (s n) -> p s n", s=2),
                                       ldt[64:96, :].unsqueeze(2).broadcast_to([32, 2, 64])), t_small)
    for i, (S, n) in enumerate(((S0, 128), (S1, 128), (S2, 112), (S3, 96))):
        tt = pe.do(lambda e, S=S, n=n, i=i: e.transpose(PS[:, 4, i * 128:i * 128 + n], S[0:n, :], ident[0:n, 0:n]), t_small, t)
    t_cols = [act.do(lambda e, n=n, i=i: e.copy(cols[:, i * 128:i * 128 + n], PS[:, 4, i * 128:i * 128 + n]), tt)
              for i, n in enumerate((128, 128, 112, 96))]
    c = cols[:, C_C:C_C + 16]
    th = dcol(8)
    ta = act.do(lambda e: e.activation(th, c, ACT.Tanh, scale=0.5), t_cols[0])
    tb = dve.do(lambda e: e.scalar_tensor_tensor(cact, th, 1.0, c, ALU.add, ALU.mult), ta)
    t_c = dve.do(lambda e: e.tensor_scalar(cact, cact, 0.5, None, ALU.mult), tb)
    tk = t_cols[1]
    dve.do(lambda e: e.tensor_scalar(dcol(3, 8), cols[:, C_BG:C_BG + 8], 0.5, None, ALU.mult), tk)
    dve.do(lambda e: e.tensor_scalar(hba, cols[:, C_BA:C_BA + 16], 0.5, None, ALU.mult), t_cols[2])
    dve.do(lambda e: e.tensor_scalar(hbx, cols[:, C_BX:C_BX + 16], 0.5, None, ALU.mult))
    lam = cols[:, C_LAM:C_LAM + 16]
    s9, s10 = dcol(9), dcol(10)
    t1 = dve.do(lambda e: e.tensor_scalar(s9, lam, -1.0, None, ALU.mult))
    t1 = dve.do(lambda e: e.tensor_tensor(s10, s9, lam, ALU.min), t1)
    t2 = act.do(lambda e: e.activation(s10, s10, ACT.Exp), t1)
    t2 = act.do(lambda e: e.activation(s10, s10, ACT.Ln, bias=1.0), t2)
    t1 = dve.do(lambda e: e.tensor_scalar(s9, s9, 0.0, None, ALU.max), t1)
    t1 = dve.do(lambda e: e.tensor_tensor(s9, s9, s10, ALU.add), t1, t2)
    t_sp = dve.do(lambda e: e.tensor_scalar(spc, s9, -4.0, None, ALU.mult), t1)

    tx = []
    xT = f3(E0 - 0, 16) if False else None
    XT = 4096
    for f2 in range(8):
        bank = 5 + f2 % 3
        for i in range(2):
            for j in range(2):
                kt = 2 * f2 + j
                o = PS[:, bank, j * T + i * P:j * T + i * P + P]
                src = xn[:, i, kt * P:(kt + 1) * P]
                tt = pe.do(lambda e, o=o, src=src: e.transpose(o, src, ident[:, :]), t_x, t_small, tx[f2 - 3] if f2 >= 3 else None)
        d = fv(XT + f2 * 512, 512)
        tx.append(dve.do(lambda e, d=d, bank=bank: e.tensor_copy(d, PS[:, bank, :]), tt))
    X3 = f3(XT, 16)
    t_xs = dma(pool, [(scr_x, fv(XT, 4096))], tx[-1])
    sqv = fv(XN, 4096)
    ss = sb("ss", [P, T])
    rstd = sb("rstd", [P, T])
    t_sq = act.do(lambda e: e.activation(sqv, fv(XT, 4096), ACT.Square), tx[-1], tt)
    t_ss = dve.do(lambda e: e.tensor_reduce(ss[:, :], sqv.rearrange("p (k n) -> p n k", k=16), AX, ALU.add), t_sq)

    def stats(bank, *tokens):
        t = pe.do(lambda e: e.matmul(PS[:, bank, 0:T], ones[:, :], ss[:, :], start=True, stop=True), t_one, *tokens)
        t = act.do(lambda e: e.activation(rstd[:, :], PS[:, bank, 0:T], ACT.Sqrt, scale=1.0 / D, bias=eps[:, 0:1]), t, t_eps)
        return dve.do(lambda e: e.reciprocal(rstd[:, :], rstd[:, :]), t)

    t_rstd = stats(5, t_ss, tx[-1])

    pw = sb("pw", [P, 12, 32])
    pv = lambda i: pw[:, i, :]
    are, aim = cols[:, C_AR:C_AR + 32], cols[:, C_AI:C_AI + 32]
    mag, ec, es, fr, fi = pv(0), pv(1), pv(2), pv(3), pv(4)
    dt_, th_, a_, b_, c_, d_, g_ = (pv(i) for i in range(5, 12))
    t0 = act.do(lambda e: e.activation(dt_, cols[:, C_LD:C_LD + 32], ACT.Exp), t_cols[3])
    t1 = dve.do(lambda e: e.tensor_tensor(a_, dt_, are, ALU.mult), t0)
    t_mag = act.do(lambda e: e.activation(mag, a_, ACT.Exp), t1)
    t1 = dve.do(lambda e: e.tensor_tensor(th_, dt_, aim, ALU.mult), t1)

    C1, C2, C3 = two_pi_parts()

    def reduce_angle(v, k, t):
        t = dve.do(lambda e: e.tensor_scalar(k, v, 1.0 / TWO_PI, MAGIC, ALU.mult, ALU.add), t)
        t = dve.do(lambda e: e.tensor_scalar(k, k, -MAGIC, None, ALU.add), t)
        for cc in (C1, C2, C3):
            t = dve.do(lambda e, cc=cc: e.scalar_tensor_tensor(v, k, -cc, v, ALU.mult, ALU.add), t)
        return dve.do(lambda e: e.tensor_scalar(v, v, 3.1415925, -3.1415925, ALU.min, ALU.max), t)

    def sincos(v, co, si, t):
        t = act.do(lambda e: e.activation(si, v, ACT.Sin), t)
        t2 = act.do(lambda e: e.activation(co, v, ACT.Sin, scale=0.5), t)
        t3 = dve.do(lambda e: e.tensor_tensor(co, co, co, ALU.mult), t2)
        return dve.do(lambda e: e.tensor_scalar(co, co, -2.0, 1.0, ALU.mult, ALU.add), t3)

    t1 = reduce_angle(th_, b_, t1)
    t_e = sincos(th_, ec, es, t1)
    t1 = dve.do(lambda e: e.tensor_tensor(a_, mag, ec, ALU.mult), t_e, t_mag)
    t1 = dve.do(lambda e: e.tensor_scalar(a_, a_, -1.0, None, ALU.add), t1)
    t2 = dve.do(lambda e: e.tensor_tensor(b_, mag, es, ALU.mult), t1)
    t3 = dve.do(lambda e: e.tensor_tensor(c_, are, are, ALU.mult))
    t4 = dve.do(lambda e: e.tensor_tensor(d_, aim, aim, ALU.mult))
    t3 = dve.do(lambda e: e.tensor_tensor(c_, c_, d_, ALU.add), t3, t4)
    t3 = dve.do(lambda e: e.reciprocal(c_, c_), t3)
    t4 = dve.do(lambda e: e.tensor_tensor(d_, a_, are, ALU.mult), t3)
    t5 = dve.do(lambda e: e.tensor_tensor(g_, b_, aim, ALU.mult), t4)
    t5 = dve.do(lambda e: e.tensor_tensor(d_, d_, g_, ALU.add), t5)
    t5 = dve.do(lambda e: e.tensor_tensor(fr, d_, c_, ALU.mult), t5)
    t6 = dve.do(lambda e: e.tensor_tensor(d_, b_, are, ALU.mult), t5)
    t6 = dve.do(lambda e: e.tensor_tensor(g_, a_, aim, ALU.mult), t6)
    t6 = dve.do(lambda e: e.tensor_tensor(d_, d_, g_, ALU.subtract), t6)
    t_f = dve.do(lambda e: e.tensor_tensor(fi, d_, c_, ALU.mult), t6)

    XB = 9600
    xb = F[:, XB:XB + 2048].rearrange("p (c t s q) -> p c t s q", c=2, t=32, s=2)
    xtmp = F[:, XB + 2048:XB + 3072].rearrange("p (c t q) -> p c t q", c=2, t=32)
    bc = lambda v: v.unsqueeze(2).broadcast_to([P, 32, 16])
    bre, bim = (bsr[:, i, :].rearrange("p (t q) -> p t q", t=32) for i in range(2))
    tz = dve.do(lambda e: e.memset(fv(XB, 2048), 0.0))
    xr_, xi_ = xtmp[:, 0], xtmp[:, 1]
    for ci in range(2):
        a, b, op = ((bre, bim, ALU.subtract), (bim, bre, ALU.add))[ci]
        t1 = dve.do(lambda e, a=a: e.tensor_tensor(xr_, a, bc(fr), ALU.mult), t_f, t_bc, tz)
        t2 = dve.do(lambda e, b=b: e.tensor_tensor(xi_, b, bc(fi), ALU.mult), t1)
        for h in range(2):
            hs = slice(64 * h, 64 * h + 64)
            tz = dve.do(lambda e, hs=hs, h=h, ci=ci, op=op: e.tensor_tensor(xb[hs, ci, :, h, :], xr_[hs], xi_[hs], op), t1, t2)
    XC = XB + 4096 + 2048 + 2048
    xc_ = F[:, CT:CT + 2048].rearrange("p (c f s n) -> p c f s n", c=2, f=8, s=2)
    for ci in range(2):
        sg = 1.0 if ci == 0 else -1.0
        for h in range(2):
            tcm = dve.do(lambda e, ci=ci, h=h, sg=sg: e.tensor_scalar(
                xc_[:, ci, :, h, :], csr[:, ci, :].rearrange("p (f n) -> p f n", f=8),
                part[:, 1 + h:2 + h], sg, ALU.mult, ALU.mult), t_bc, t_hot)
    lb = F[:, LB:LB + 2048].rearrange("p (c f s) -> p c f s", c=2, f=8)
    ct = F[:, CT:CT + 2048].rearrange("p (c f s) -> p c f s", c=2, f=8)
    tlc = [None]
    tl = [None, None]
    xb2 = F[:, XB:XB + 2048].rearrange("p (c f s) -> p c f s", c=2, f=8)
    n = 0
    for src, dst, tok in ((xb2, lb, tz), (ct, ct, tcm)):
        for ci in range(2):
            for half in range(2):
                bank = 6 + n % 2
                for j in range(4):
                    tt = pe.do(lambda e, bank=bank, j=j, ci=ci, half=half, src=src: e.transpose(
                        PS[:, bank, j * P:j * P + P], src[:, ci, 4 * half + j, :], ident[:, :]), tok, tl[n % 2], tx[-1])
                d = dst[:, ci, 4 * half:4 * half + 4, :]
                tl[n % 2] = act.do(lambda e, d=d, bank=bank: e.copy(d, PS[:, bank, :].rearrange("p (a n) -> p a n", a=4)), tt, tz, t_bc)
                n += 1
    t_lc = tl[:]

    tt = pe.do(lambda e: e.matmul(PS[0:8, 4, 0:384], relb[0:32, :], hot[0:32, :], start=True, stop=True), t_hot, t_cols[-1])
    t1 = dve.do(lambda e: e.tensor_tensor(negr[0:8, :], PS[0:8, 4, 0:384], negr[0:8, :], ALU.add), tt)
    t_bs = dma(pool, [(scr_b, negr[0:8, :])], t1)
    t_setup_free = [t_bs, t_xs, t_lc[0], t_lc[1]]

    wada = w2("w_ada")
    adat = [None]

    def ada_pe(q, kt):
        def use(r, tok):
            for j in range(8):
                cidx = q * 8 + j
                f = lambda e, j=j, cidx=cidx: e.matmul(PS[:, 0, cidx:cidx + 1], r[:, j * P:(j + 1) * P], cact[:, kt:kt + 1],
                                                       start=(kt == 0 and q == 0 and j == 0), stop=(kt == 15),
                                                       skip_group_check=True)
                if j == 7:
                    adat[0] = pe.do(f, tok, t_c)
                else:
                    pe.quiet(f, tok, t_c)
            return adat[0]
        return use

    for kt in range(16):
        for q in range(4):
            add_ada(wada[kt * P:(kt + 1) * P, q * 1024:(q + 1) * 1024].rearrange("p (k n) -> p k n", k=1), ada_pe(q, kt))

    waitfor, done = {}, {}

    aacc = sb("aacc", [P, 1024])
    mod_ready = {}
    ada_prev = [None]

    def ada_dve(g, q, kt):
        def use(r, tok):
            a = aacc[:, :]
            if kt == 0:
                t = dve.do(lambda e: e.tensor_scalar(a, r, cact[:, 0:1], None, ALU.mult), tok, t_c, ada_prev[0])
            else:
                t = dve.do(lambda e: e.scalar_tensor_tensor(a, r, cact[:, kt:kt + 1], a, ALU.mult, ALU.add), tok, ada_prev[0])
            ada_prev[0] = t
            if kt == 15:
                mod_ready[(g, q)] = t
            return t
        return use

    mfree = {4: None, 5: None, 6: None, 7: None}

    def ada_close(g, q, bank=7):
        for j in range(8):
            t = pe.do(lambda e, j=j: e.matmul(PS[:, bank, j:j + 1], aacc[:, j * P:(j + 1) * P], ones[:, 0:1],
                                              start=(j == 0), stop=(j == 7), skip_group_check=True),
                      mod_ready[(g, q)], mfree[bank])
        o = g * 16 + q * 8
        t2 = dve.do(lambda e: e.tensor_tensor(mod[:, o:o + 8], PS[:, bank, 0:8], cols[:, C_BADA + o:C_BADA + o + 8], ALU.add), t)
        mfree[bank] = [t2]
        ada_prev[0] = [t2]
        done["mod%d%d" % (g, q)] = t2

    def add_ada_group(g, q):
        for kt in range(16):
            c0 = g * D + q * 1024
            yield (wada[kt * P:(kt + 1) * P, c0:c0 + 1024].rearrange("p (k n) -> p k n", k=1), ada_dve(g, q, kt))

    tmp = f3(3072, 3)
    tmpf = [None, None, None]

    def apply_norm(src3, gain, shift, op, *tokens):
        for k in range(16):
            s = k % 3
            tv = tmp[:, s, :]
            a = dve.do(lambda e, k=k, tv=tv: e.scalar_tensor_tensor(tv, src3[:, k, :], gain[:, k:k + 1], rstd[:, :], ALU.mult, ALU.mult),
                       tmpf[s], *tokens)
            if shift is None:
                b = act.do(lambda e, k=k, tv=tv: e.activation(op.hi(k), tv, ACT.Copy), a, *tokens)
                t = dve.do(lambda e, k=k, tv=tv: e.tensor_tensor(op.lo(k), tv, op.hi(k).bitcast(F32), ALU.subtract), b)
            else:
                b = act.do(lambda e, k=k, tv=tv: e.activation(op.hi(k), tv, ACT.Identity, bias=shift[:, k:k + 1]), a, *tokens)
                t = dve.do(lambda e, k=k, tv=tv: e.scalar_tensor_tensor(op.lo(k), tv, shift[:, k:k + 1], op.hi(k).bitcast(F32),
                                                                        ALU.add, ALU.subtract), b)
            tmpf[s] = t
            op.ready[k] = t
        return t

    sqt = fv(2048, 1024)
    ssf = {"t": None, "sq": None, "use": None}

    def add_squares(src, p, *tokens):
        a = act.do(lambda e: e.activation(sqt, src, ACT.Square), ssf["sq"], *tokens)
        v = sqt.rearrange("p (k n) -> p n k", k=4)
        if p == 0:
            t = dve.do(lambda e: e.tensor_reduce(ss[:, :], v, AX, ALU.add), a, ssf["use"])
        else:
            t = dve.do(lambda e: e.tensor_reduce(tmp[:, 0, :], v, AX, ALU.add), a, tmpf[0])
            t = dve.do(lambda e: e.tensor_tensor(ss[:, :], ss[:, :], tmp[:, 0, :], ALU.add), t, ssf["t"])
            tmpf[0] = t
        ssf["sq"] = t
        ssf["t"] = t
        return t

    h = Operand(0, 1)
    yg = Operand(2)
    ys = Operand(3)
    ya = Operand(0)
    mg = Operand(1, 2)
    h2 = Operand(0, 3)
    hid = Operand(1, 2)

    w_in = w2("w_in")
    u3 = f3(U, 8)
    ureadt = {}
    tokens_kv = {}

    def ev_copy(dst, name, eng="act"):
        def ev(full, t):
            if eng == "act":
                r = act.do(lambda e: e.copy(dst, full), t, *waitfor.get(name, []))
            else:
                r = dve.do(lambda e: e.tensor_copy(dst, full), t, *waitfor.get(name, []))
            done[name] = r
            return [r]
        return ev

    def ev_tanh(dst, name):
        def ev(full, t):
            r = act.do(lambda e: e.activation(dst, full, ACT.Tanh, scale=0.5), t, *waitfor.get(name, []))
            done[name] = r
            return [r]
        return ev

    ssw = F[:, SW:SW + 3072].rearrange("p (r b c n) -> p r b c n", r=2, b=3, c=2)
    sst = {"wfree": [None, None], "pool": [None, None]}
    ytok = {}

    def etable(ft):
        b = ft % 2
        Ec = f3(E0 + b * 2048, 4)
        Es = f3(E0 + b * 2048 + 1024, 4)
        return Ec, Es

    e_ready, e_free = {}, {}

    def make_e(ft, sw):
        Ec, Es = etable(ft)
        tt = ft * 4
        w0 = e_free.get(ft - 2)
        t = pool.do(lambda e: e.memset(Ec[:, :, 0:1], 1.0), w0, *t_setup_free)
        t = pool.do(lambda e: e.memset(Es[:, :, 0:1], 0.0), t)
        t = pool.do(lambda e: e.tensor_copy(Ec[:, :, 1:2], ec[:, tt:tt + 4].unsqueeze(2)), t, t_e)
        t = pool.do(lambda e: e.tensor_copy(Es[:, :, 1:2], es[:, tt:tt + 4].unsqueeze(2)), t)
        n = 1
        while n < T:
            m = n
            if n > 1:
                pass
            cr, ci_ = Ec[:, :, n:n + 1].broadcast_to([P, 4, m]), Es[:, :, n:n + 1].broadcast_to([P, 4, m])
            A = scre[:, :, 0:m]
            if n > 1 or True:
                lo = 1
                cnt = min(m, T - n) - 1
                if cnt > 0:
                    crn = Ec[:, :, n:n + 1].broadcast_to([P, 4, cnt])
                    cin = Es[:, :, n:n + 1].broadcast_to([P, 4, cnt])
                    s0, s1 = Ec[:, :, 1:1 + cnt], Es[:, :, 1:1 + cnt]
                    d0, d1 = Ec[:, :, n + 1:n + 1 + cnt], Es[:, :, n + 1:n + 1 + cnt]
                    A = scre[:, :, 0:cnt]
                    t1 = pool.do(lambda e, A=A, s1=s1, cin=cin: e.tensor_tensor(A, s1, cin, ALU.mult), t)
                    t2 = pool.do(lambda e, d0=d0, s0=s0, crn=crn: e.tensor_tensor(d0, s0, crn, ALU.mult), t)
                    t3 = pool.do(lambda e, A=A, d0=d0: e.tensor_tensor(d0, d0, A, ALU.subtract), t1, t2)
                    t4 = pool.do(lambda e, A=A, s0=s0, cin=cin: e.tensor_tensor(A, s0, cin, ALU.mult), t3)
                    t5 = pool.do(lambda e, d1=d1, s1=s1, crn=crn: e.tensor_tensor(d1, s1, crn, ALU.mult), t3)
                    t = pool.do(lambda e, A=A, d1=d1: e.tensor_tensor(d1, d1, A, ALU.add), t4, t5)
                if 2 * n < T:
                    c0, c1 = Ec[:, :, n:n + 1], Es[:, :, n:n + 1]
                    e0, e1 = Ec[:, :, 2 * n:2 * n + 1], Es[:, :, 2 * n:2 * n + 1]
                    A = scre[:, :, 0:1]
                    t1 = pool.do(lambda e, A=A, c1=c1: e.tensor_tensor(A, c1, c1, ALU.mult), t)
                    t2 = pool.do(lambda e, e0=e0, c0=c0: e.tensor_tensor(e0, c0, c0, ALU.mult), t)
                    t3 = pool.do(lambda e, A=A, e0=e0: e.tensor_tensor(e0, e0, A, ALU.subtract), t1, t2)
                    t4 = pool.do(lambda e, A=A, c0=c0, c1=c1: e.tensor_tensor(A, c0, c1, ALU.mult), t3)
                    t = pool.do(lambda e, A=A, e1=e1: e.tensor_tensor(e1, A, A, ALU.add), t4)
            n *= 2
        e_ready[ft] = t

    scre = sb("scre", [P, 4, P])

    def ssm_task():
        for ft in range(8):
            if ft == 0:
                make_e(0, 0)
                make_e(1, 0)
            elif ft + 1 < 8:
                make_e(ft + 1, 0)
            Ec, Es = etable(ft)
            yb = 6
            for j in range(4):
                tl_ = 4 * ft + j
                bank = 4 + tl_ % 2
                rs = slice(32 * j, 32 * j + 32)
                w0 = done["u%d" % (ft // 4)]
                for ci in range(2):
                    tb_ = pe.do(lambda e, ci=ci, bank=bank, rs=rs, ft=ft: e.matmul(
                        PS[:, bank, ci * T:ci * T + T], lb[rs, ci, ft, :], u3[rs, ft, :], start=True, stop=True),
                        mfree[bank], w0, *t_lc)
                yield
                r = tl_ % 2
                m1, m2, m3 = (ssw[:, r, i] for i in range(3))
                bu = PS[:, bank, :].rearrange("p (c n) -> p c n", c=2)
                cc, sn = Ec[:, j, :], Es[:, j, :]
                ccb = cc.unsqueeze(1).broadcast_to([P, 2, T])
                x1 = dve.do(lambda e: e.tensor_tensor(m1, bu, ccb, ALU.mult), tb_, e_ready[ft], sst["pool"][r])
                x2 = dve.do(lambda e: e.tensor_tensor(m2[:, 0, :], bu[:, 1, :], sn, ALU.mult))
                x3 = dve.do(lambda e: e.tensor_tensor(m2[:, 1, :], bu[:, 0, :], sn, ALU.mult))
                mfree[bank] = [x3]
                x4 = dve.do(lambda e: e.tensor_tensor(m1[:, 0, :], m1[:, 0, :], m2[:, 0, :], ALU.add), x1, x2)
                x5 = dve.do(lambda e: e.tensor_tensor(m1[:, 1, :], m1[:, 1, :], m2[:, 1, :], ALU.subtract), x3)
                dec = mag[:, tl_:tl_ + 1].broadcast_to([P, T])
                x6 = dve.do(lambda e: e.tensor_tensor_scan(m2[:, 0, :], dec, m1[:, 0, :], 0.0, ALU.mult, ALU.add), x4)
                x7 = dve.do(lambda e: e.tensor_tensor_scan(m2[:, 1, :], dec, m1[:, 1, :], 0.0, ALU.mult, ALU.add), x5)
                snb = sn.unsqueeze(1).broadcast_to([P, 2, T])
                y1 = pool.do(lambda e: e.tensor_tensor(m1, m2, ccb, ALU.mult), x6, x7)
                y2 = pool.do(lambda e: e.tensor_tensor(m3, m2, snb, ALU.mult), x6, x7)
                y3 = pool.do(lambda e: e.tensor_tensor(m1[:, 0, :], m1[:, 0, :], m3[:, 1, :], ALU.subtract), y1, y2)
                y4 = pool.do(lambda e: e.tensor_tensor(m1[:, 1, :], m1[:, 1, :], m3[:, 0, :], ALU.add), y1, y2)
                if j == 3:
                    e_free[ft] = [y2]
                yield
                for ci in range(2):
                    ty = pe.do(lambda e, ci=ci, j=j, ft=ft, yb=yb, m1=m1: e.matmul(
                        PS[32 * j:32 * j + 32, yb, 0:T], ct[:, ci, ft, 32 * j:32 * j + 32], m1[:, ci, :],
                        start=(ci == 0), stop=(ci == 1)), y3, y4, mfree[yb])
                sst["pool"][r] = ty
            yv = PS[:, yb, 0:T]
            v, g1_ = gtmp[:, 0, :], gtmp[:, 1, :]
            z1 = dve.do(lambda e, ft=ft: e.scalar_tensor_tensor(v, u3[:, ft, :], cols[:, C_SD + ft:C_SD + ft + 1], yv, ALU.mult, ALU.add), ty)
            mfree[yb] = [z1]
            z2 = act.do(lambda e: e.activation(g1_, v, ACT.Square), z1)
            z3 = dve.do(lambda e: e.tensor_scalar(g1_, g1_, GELU_A, 1.0, ALU.mult, ALU.add), z2)
            z4 = dve.do(lambda e: e.tensor_tensor(g1_, g1_, v, ALU.mult), z3)
            z5 = act.do(lambda e: e.activation(g1_, g1_, ACT.Tanh, scale=GELU_C), z4)
            z6 = dve.do(lambda e: e.scalar_tensor_tensor(v, g1_, 1.0, v, ALU.add, ALU.mult), z5)
            split_out(yg, ft, 1, v, 0.5, z6)
            yield
        return

    gtmp = sb("gtmp", [P, 2, T])

    q3, k3, v3 = f3(Q, 8), f3(K, 8), f3(V, 8)
    bh = f3(BH, 8)
    awv = F[:, AW:AW + 3 * 772].rearrange("p (r n) -> p r n", r=3)
    vn = f3(U, 2, 1024)
    SCALE1 = 128.0 ** -0.5
    atf = [None, None, None]

    def attn_head(hd, t_b):
        r = hd % 3
        w = awv[:, r, :]
        s_, pt = w[:, 0:384], w[:, 384:768]
        mx, sm = w[:, 768:770], w[:, 770:772]
        ba = 4 + r
        tq = [done["q%d" % (hd // 4)], done["k%d" % (hd // 4)]]
        p1 = pe.do(lambda e: e.matmul(PS[:, ba, 0:256], q3[:, hd, 128:256], k3[:, hd, :], start=True, stop=True), tq, mfree[ba])
        p1 = pe.do(lambda e: e.matmul(PS[:, ba, 256:384], q3[:, hd, 0:128], k3[:, hd, 0:128], start=True, stop=True))
        yield
        d1 = dve.do(lambda e: e.scalar_tensor_tensor(s_[:, 0:256], PS[:, ba, 0:256], SCALE1, bh[:, hd, :], ALU.mult, ALU.add), p1, t_b, atf[r])
        d2 = dve.do(lambda e: e.scalar_tensor_tensor(s_[:, 256:384], PS[:, ba, 256:384], SCALE1, bh[:, hd, 128:256], ALU.mult, ALU.add))
        d3 = dve.do(lambda e: e.tensor_reduce(mx[:, 0:1], s_[:, 0:256], AX, ALU.max, negate=True), d1)
        d4 = dve.do(lambda e: e.tensor_reduce(mx[:, 1:2], s_[:, 256:384], AX, ALU.max, negate=True), d2)
        a1 = act.do(lambda e: e.activation(s_[:, 0:256], s_[:, 0:256], ACT.Exp, bias=mx[:, 0:1], accum_out=sm[:, 0:1]), d3)
        a2 = act.do(lambda e: e.activation(s_[:, 256:384], s_[:, 256:384], ACT.Exp, bias=mx[:, 1:2], accum_out=sm[:, 1:2]), d4)
        yield
        d5 = dve.do(lambda e: e.reciprocal(sm, sm), a1, a2)
        d6 = dve.do(lambda e: e.tensor_scalar(s_[:, 0:256], s_[:, 0:256], sm[:, 0:1], None, ALU.mult), d5)
        d7 = dve.do(lambda e: e.tensor_scalar(s_[:, 256:384], s_[:, 256:384], sm[:, 1:2], None, ALU.mult), d5)
        yield
        for src, dst in ((256, 0), (0, 128), (128, 256)):
            p3 = pe.do(lambda e, src=src, dst=dst: e.transpose(PS[:, ba, dst:dst + P], s_[:, src:src + P], ident[:, :]), d6, d7)
        a3 = act.do(lambda e: e.copy(pt, PS[:, ba, 0:384]), p3)
        yield
        vh = slice(hd * P, hd * P + P)
        pe.quiet(lambda e: e.matmul(PS[:, ba, 0:256], vn[:, 0, vh], pt[:, 0:256], start=True, stop=False, skip_group_check=True), a3, done["vn"])
        p4 = pe.do(lambda e: e.matmul(PS[:, ba, 128:256], vn[:, 1, vh], pt[:, 256:384], start=False, stop=True, skip_group_check=True))
        atf[r] = p4
        yield
        t = split_out(ya, hd, 1, PS[:, ba, 0:256], 1.0, p4, h_free[0])
        mfree[ba] = [t]

    h_free = [None]
    tbias = [None]

    def attn_task():
        for i in range(4):
            bank = 4 + i % 2
            t = pe.do(lambda e: e.matmul(PS[:, bank, :], fv(AW + 2320, P), fv(AW + i * 512, 512), start=True, stop=True),
                      tbias[0], mfree[bank])
            t = act.do(lambda e: e.copy(fv(BH + i * 512, 512), PS[:, bank, :]), t)
            mfree[bank] = [t]
        t_b = t
        atf[0] = atf[1] = atf[2] = t
        yield
        for i in range(2):
            for g in range(2):
                bank = 4 + g
                for hd in range(4 * g, 4 * g + 4):
                    t = pe.do(lambda e, i=i, hd=hd, bank=bank: e.transpose(PS[:, bank, (hd % 4) * P:(hd % 4) * P + P],
                                                                          v3[:, hd, i * P:i * P + P], ident[:, :]),
                              done["v0"], done["v1"], mfree[bank])
                t = act.do(lambda e, i=i, g=g, bank=bank: e.copy(vn[:, i, g * 512:g * 512 + 512], PS[:, bank, :]), t)
                mfree[bank] = [t]
        done["vn"] = t
        yield
        for lot in ((0, 1, 2), (3, 4, 5), (6, 7)):
            g = [attn_head(hd, t_b) for hd in lot]
            while g:
                for x in list(g):
                    try:
                        next(x)
                    except StopIteration:
                        g.remove(x)
                yield

    runs = []

    def panel(W, k0, nkt, c0, operand, evac, before=None, bg=1):
        srcs, mms = std(W, k0, nkt, c0)
        p = add_panel(srcs, 2, mms, operand, evac, before, bg)
        runs.append(p)
        return p

    def call(f):
        runs.append(f)

    def start_h():
        t = dve.do(lambda e: e.tensor_tensor(mod[:, 0:32], PS[:, 0, 0:32], cols[:, C_BADA:C_BADA + 32], ALU.add), adat[0])
        t = dve.do(lambda e: e.scalar_tensor_tensor(A1, mod[:, 16:32], 1.0, cols[:, C_G1:C_G1 + 16], ALU.add, ALU.mult), t)
        gfree[0] = [t]
        apply_norm(X3, A1, mod[:, 0:16], h, t, t_rstd)

    call(lambda: (advance(63), start_h()))
    for p in range(2):
        panel(w_in, 0, 16, p * 512, h, ev_copy(fv(U + p * 1024, 1024), "u%d" % p))
        if p == 0:
            call(lambda: background.append(ssm_task()))
            waitfor["u0"] = waitfor["u1"] = t_setup_free

    def early_gates():
        waitfor["ga0"] = [h.ready[15], t_sq]

    call(early_gates)
    for i in range(4):
        panel(w_in, 0, 16, 4096 + i * 512, h, ev_tanh(fv(GA + i * 1024, 1024), "ga%d" % i), bg=2)
    for i in range(4):
        panel(w_in, 0, 16, 6144 + i * 512, h, ev_tanh(fv(GB + i * 1024, 1024), "gb%d" % i), bg=2)

    def ssm_end():
        while background:
            step()
        last = [(dve.sem, dve.n), (pool.sem, pool.n), (pe.sem, pe.n)]
        waitfor["q0"] = last

    call(ssm_end)
    for nm, cb, dst in (("q", 1024, Q), ("k", 2048, K), ("v", 3072, V)):
        for i in range(2):
            panel(w_in, 0, 16, cb + i * 512, h, ev_copy(fv(dst + i * 1024, 1024), "%s%d" % (nm, i)))

    def after_w_in():
        h_free[0] = (pe.sem, pe.n)
        base = scr_b
        pairs = [(fv(AW + 2320, P), I["c_swap"][:, P:2 * P])]
        for hd in range(8):
            src = bass.AP(tensor=base.tensor, offset=base.offset + hd * 384, ap=[[1, P], [1, T]])
            pairs.append((fv(AW + hd * T, T), src))
        tbias[0] = dma(pool, pairs, t_bs, (dve.sem, dve.n), (pe.sem, pe.n), (act.sem, act.n))
        background.append(attn_task())

    call(after_w_in)

    def ev_glu(p):
        def ev(full, t):
            for m in range(4):
                k = 4 * p + m
                v, g1_ = gtmp[:, 0, :], gtmp[:, 1, :]
                pm = full[:, m * T:m * T + T]
                a = act.do(lambda e, k=k, pm=pm: e.activation(g1_, pm, ACT.Tanh, scale=0.5, bias=hbg[:, k:k + 1]), t, ys.ready[k - 1] if k else None)
                b = dve.do(lambda e, k=k: e.tensor_tensor(v, yg.hi(k).bitcast(F32), yg.lo(k).bitcast(F32), ALU.add), ys.ready[k - 1] if k else None)
                b = dve.do(lambda e: e.scalar_tensor_tensor(v, g1_, 1.0, v, ALU.add, ALU.mult), a, b)
                split_out(ys, k, 1, v, 0.5, b)
            return [a]
        return ev

    w_glu = w2("w_glu")
    for p in range(2):
        panel(w_glu, 0, 8, p * 512, yg, ev_glu(p), bg=2)

    def ev_gate1(off, name):
        def ev(full, t):
            g = fv(off, 1024)
            r = dve.do(lambda e: e.scalar_tensor_tensor(g, g, 1.0, full, ALU.add, ALU.mult), t)
            done[name] = r
            return [r]
        return ev

    def ev_gate2(off, off1, op, k, name, free):
        def ev(full, t):
            g = fv(off, 1024)
            r = dve.do(lambda e: e.scalar_tensor_tensor(g, g, 1.0, full, ALU.add, ALU.mult), t)
            r2 = dve.do(lambda e: e.tensor_tensor(g, g, fv(off1, 1024), ALU.add), r)
            split_out(op, k, 4, g, 0.5, r2, *free())
            return [r]
        return ev

    wps, wpa = w2("w_proj_ssm"), w2("w_proj_attn")
    for i in range(4):
        panel(wps, 0, 8, i * 512, ys, ev_gate1(GA + i * 1024, "ps%d" % i), bg=2)

    def attn_end():
        while background:
            step()

    call(attn_end)
    XR = 10240
    xr3 = f3(XR, 16)
    t_x2 = [None]

    def reload_x():
        t_x2[0] = dma(pool, [(fv(XR, 4096), scr_x)], t_xs, (pe.sem, pe.n), (act.sem, act.n), (dve.sem, dve.n))

    call(reload_x)
    for i in range(4):
        panel(wpa, 0, 8, i * 512, ya, ev_gate2(GB + i * 1024, GA + i * 1024, mg, 4 * i, "pa%d" % i, lambda: [h_free[0]]))

    def ev_res(dst3, p, gcol, need, final=True):
        def ev(full, t):
            for m in range(4):
                k = 4 * p + m
                r = dve.do(lambda e, k=k, m=m: e.scalar_tensor_tensor(dst3[:, k, :], full[:, m * T:m * T + T], gcol[:, k:k + 1],
                                                                     dst3[:, k, :], ALU.mult, ALU.add), t, t_x2[0], done[need])
            if final:
                add_squares(dst3[:, 4 * p:4 * p + 4, :].rearrange("p k n -> p (k n)"), p, r)
            return [r]
        return ev

    resw = []
    w_out = w2("w_out")

    for i in range(4):
        panel(w_out, 0, 16, i * 512, mg, ev_res(xr3, i, mod[:, 32:48], "mod21"))

    def norm2():
        t = dve.do(lambda e: e.scalar_tensor_tensor(A2, mod[:, 64:80], 1.0, cols[:, C_GM:C_GM + 16], ALU.add, ALU.mult),
                   done["mod41"])
        ts = stats(4, ssf["t"], mfree[4])
        ssf["use"] = ts
        apply_norm(xr3, A2, mod[:, 48:64], h2, t, ts, done["mod31"], (pe.sem, pe.n))

    call(norm2)

    def ffn(W1, W2, src, hid, ev2, tag):
        for ch in range(4):
            for i in range(4):
                def ev(full, t, i=i):
                    r = ffr[:, i % 2, :]
                    a = act.do(lambda e: e.activation(r, full, ACT.Relu), t, fff[i % 2])
                    b = dve.do(lambda e: e.tensor_tensor(r, r, r, ALU.mult), a)
                    fff[i % 2] = split_out(hid, 4 * i, 4, r, 1.0, b)
                    return [a]
                panel(W1, 0, 16, ch * 2048 + i * 512, src, ev)
            for i in range(4):
                panel(W2, ch * 16, 16, i * 512, hid, ev2(ch, i))

    FFR = 0
    ffr = F[:, FFR:FFR + 2048].rearrange("p (r n) -> p r n", r=2)
    fff = [None, None]
    ffn(w2("w_ff1"), w2("w_ff2"), h2, hid, lambda ch, i: ev_res(xr3, i, mod[:, 80:96], "mod51", ch == 3), "1")

    H = Operand(0, 3)
    xc = Operand(1, 2)
    yr_op = xc
    YA = Operand(0, 3)
    MG = Operand(1, 2)
    H2 = Operand(0, 3)
    HID = Operand(1, 2)
    XC = 0
    Q2 = 4096
    KK = 14336
    VN = 15360
    VT = 18432
    ROT = 16384
    W8 = 18432
    cosb, sinb, nz, zz = (fv(ROT + i * 256, 256) for i in range(4))
    AWK = ROT + 1024
    invf = part[:, 0:1]
    msk = fv(8192, 256)
    swp = fv(8448, 128)
    sink = fv(8576, 32)
    esk = fv(8608, 32)
    rot = {}

    def rope_task():
        pos = sinb.bitcast(I32)
        free = [(pe.sem, pe.n), (dve.sem, dve.n), (act.sem, act.n), (pool.sem, pool.n)]
        t = dma(pool, [(pos, I["positions_2"][0:1, :].broadcast_to([P, T])),
                       (msk, I["c_mask"]), (swp, I["c_swap"][:, 0:P]),
                       (sink, I["attn_sinks_2"][0:1, :].broadcast_to([P, 32]))], *free)
        rot["sink"] = t
        pf = zz
        kk = nz
        t1 = dve.do(lambda e: e.tensor_copy(pf, pos), t, *free)
        t1 = dve.do(lambda e: e.tensor_scalar(sinb, pf, invf, None, ALU.mult), t1)
        t1 = reduce_angle(sinb, kk, t1)
        yield
        t2 = act.do(lambda e: e.activation(cosb, sinb, ACT.Sin, scale=0.5), t1)
        t2 = act.do(lambda e: e.activation(sinb, sinb, ACT.Sin), t2)
        t3 = dve.do(lambda e: e.tensor_tensor(cosb, cosb, cosb, ALU.mult), t2)
        t3 = dve.do(lambda e: e.tensor_scalar(cosb, cosb, -2.0, 1.0, ALU.mult, ALU.add), t3)
        t4 = dve.do(lambda e: e.tensor_scalar(nz, pf, 0.0, None, ALU.not_equal), t1)
        t4 = dve.do(lambda e: e.tensor_scalar(zz, pf, 0.0, None, ALU.is_equal), t4)
        rot["t"] = [t3, t4]
        yield

    call(lambda: background.append(rope_task()))

    def norm3():
        while background:
            step()
        ts = stats(4, ssf["t"], mfree[4])
        ssf["use"] = ts
        gf = cols[:, C_GF:C_GF + 16]
        for p in range(4):
            for k in range(4 * p, 4 * p + 4):
                r = dve.do(lambda e, k=k: e.scalar_tensor_tensor(xr3[:, k, :], xr3[:, k, :], gf[:, k:k + 1], rstd[:, :], ALU.mult, ALU.mult), ts)
            add_squares(xr3[:, 4 * p:4 * p + 4, :].rearrange("p k n -> p (k n)"), p, r)
        ts = stats(4, ssf["t"], r)
        ssf["use"] = ts
        apply_norm(xr3, cols[:, C_PRE:C_PRE + 16], None, H, ts, (pe.sem, pe.n))
        resw.append((dve.sem, dve.n))

    call(norm3)
    win2 = w2("w_in_2")
    xc3 = f3(XC, 16)
    cw = lambda w, k: cols[:, C_CW + 16 * w + k:C_CW + 16 * w + k + 1]

    def ev_conv(p):
        def ev(full, t):
            for m in range(4):
                k = 4 * p + m
                a = act.do(lambda e, k=k, m=m: e.activation(xc3[:, k, :], full[:, m * T:m * T + T], ACT.Identity, scale=cw(3, k),
                                                            bias=cols[:, C_CB + k:C_CB + k + 1]), t, *resw)
            a0 = a
            for m in range(4):
                k = 4 * p + m
                pm = full[:, m * T:m * T + T]
                y = xc3[:, k, :]
                a = a0
                for d in (1, 2, 3):
                    a = dve.do(lambda e, k=k, d=d, pm=pm, y=y: e.scalar_tensor_tensor(y[:, d:T], pm[:, 0:T - d], cw(3 - d, k), y[:, d:T],
                                                                                     ALU.mult, ALU.add), a)
            split_out(xc, 4 * p, 4, fv(XC + 1024 * p, 1024), 1.0, a)
            return [a]
        return ev

    for i in range(4):
        panel(win2, 0, 16, i * 512, H, ev_conv(i))

    GW = 16384 + 1024
    gA = fv(GW, 1024)
    gM = fv(GW + 1024, 1024)
    gX = fv(GW + 2048, 1024)
    gT = {"x": None}

    def rg_panel(name, p, ev):
        v = I[name].rearrange("o b (k p) j -> p (o b k) j", p=P)
        srcs = [v[:, 4 * p:4 * p + 4, :]]
        mms = lambda u: [(b * 512 + kk * 256 + jt * P, 4 * p + 2 * b + kk, 2 * b + jt)
                         for b in range(2) for jt in range(2) for kk in range(2)]
        x = add_panel(srcs, 4, mms, xc, ev)
        runs.append(x)

    def ev_ra(p):
        def ev(full, t):
            for m in range(4):
                k = 4 * p + m
                o = gA[:, m * T:m * T + T]
                a = act.do(lambda e, k=k, m=m, o=o: e.activation(o, full[:, m * T:m * T + T], ACT.Tanh, scale=0.5, bias=hba[:, k:k + 1]), t, gT["x"])
                b = dve.do(lambda e, k=k, o=o: e.tensor_scalar(o, o, 1.0, spc[:, k:k + 1], ALU.add, ALU.mult), a, t_sp)
            c1 = act.do(lambda e: e.activation(gM, gA, ACT.Tanh, scale=-1.0), b, gT["x"])
            c2 = act.do(lambda e: e.activation(gA, gA, ACT.Exp), b)
            d1 = dve.do(lambda e: e.tensor_scalar(gX, gM, 1.0, None, ALU.add), c1, gT["x"])
            d1 = dve.do(lambda e: e.reciprocal(gX, gX), d1)
            d1 = dve.do(lambda e: e.scalar_tensor_tensor(gM, gM, 2.0, gX, ALU.mult, ALU.mult), d1)
            c3 = act.do(lambda e: e.activation(gM, gM, ACT.Sqrt), d1)
            nb = lambda v: v.unsqueeze(1).broadcast_to([P, 4, T])
            g3 = lambda v: v.rearrange("p (k n) -> p k n", k=4)
            d2 = dve.do(lambda e: e.tensor_tensor(g3(gA), g3(gA), nb(nz), ALU.mult), c2)
            d3 = dve.do(lambda e: e.tensor_tensor(g3(gM), g3(gM), nb(nz), ALU.mult), c3)
            d4 = dve.do(lambda e: e.tensor_tensor(g3(gM), g3(gM), nb(zz), ALU.add), d3)
            gT["m"] = [d2, d4]
            gT["r"] = d1
            return [a]
        return ev

    def ev_rx(p):
        def ev(full, t):
            for m in range(4):
                k = 4 * p + m
                o = gX[:, m * T:m * T + T]
                a = act.do(lambda e, k=k, m=m, o=o: e.activation(o, full[:, m * T:m * T + T], ACT.Tanh, scale=0.5, bias=hbx[:, k:k + 1]), t, gT["r"])
            xv = fv(XC + 1024 * p, 1024)
            b = dve.do(lambda e: e.scalar_tensor_tensor(gX, gX, 1.0, xv, ALU.add, ALU.mult), a)
            b = dve.do(lambda e: e.scalar_tensor_tensor(gX, gX, 0.5, gM, ALU.mult, ALU.mult), b, gT["m"])
            for m in range(4):
                k = 4 * p + m
                sl = slice(m * T, m * T + T)
                c = dve.do(lambda e, k=k, sl=sl: e.tensor_tensor_scan(xc3[:, k, :], gA[:, sl], gX[:, sl], 0.0, ALU.mult, ALU.add), b)
            gT["x"] = c
            return [a]
        return ev

    yt = {"x": None}

    def ev_yr(p):
        def ev(full, t):
            g = gY
            a = act.do(lambda e: e.activation(g, full, ACT.Square), t, yt["x"])
            b = dve.do(lambda e: e.tensor_scalar(g, g, GELU_A, 1.0, ALU.mult, ALU.add), a)
            b = dve.do(lambda e: e.tensor_tensor(g, g, full, ALU.mult), b)
            c = act.do(lambda e: e.activation(g, g, ACT.Tanh, scale=GELU_C), b)
            d = dve.do(lambda e: e.scalar_tensor_tensor(g, g, 1.0, full, ALU.add, ALU.mult), c)
            d2 = dve.do(lambda e: e.scalar_tensor_tensor(g, g, 0.5, fv(XC + 1024 * p, 1024), ALU.mult, ALU.mult), d)
            yt["x"] = split_out(xc, 4 * p, 4, g, 1.0, d2, rgdone[p])
            return [d]
        return ev

    gY = fv(9216, 1024)
    rgdone = {}
    for i in range(4):
        rg_panel("w_rg_a_2", i, ev_ra(i))
        rg_panel("w_rg_x_2", i, ev_rx(i))
        call(lambda i=i: rgdone.update({i: (pe.sem, pe.n)}))
        panel(win2, 0, 16, 2048 + i * 512, H, ev_yr(i))

    qtmp = gA

    def rope(dst, full, n, t, *more):
        a = act.do(lambda e: e.copy(dst, full), t, *more)
        for m in range(n):
            bank = 4 + m // 2
            b = pe.do(lambda e, m=m, bank=bank: e.matmul(PS[:, bank, (m % 2) * T:(m % 2) * T + T], swp, dst[:, m * T:m * T + T],
                                                         start=True, stop=True), a, mfree[4], mfree[5], rot["sink"])
        nb = lambda v: v.unsqueeze(1).broadcast_to([P, n, T])
        d3 = dst.rearrange("p (k n) -> p k n", k=n)
        t3 = qtmp[:, 0:n * T].rearrange("p (k n) -> p k n", k=n)
        sw3 = PS[:, 4:6, :].rearrange("p a n -> p (a n)")[:, 0:n * T].rearrange("p (k n) -> p k n", k=n)
        c = dve.do(lambda e: e.tensor_tensor(t3, sw3, nb(sinb), ALU.mult), b, gT["x"], rot["t"])
        mfree[4] = [c]
        mfree[5] = [c]
        d = dve.do(lambda e: e.tensor_tensor(d3, d3, nb(cosb), ALU.mult), b)
        return a, dve.do(lambda e: e.tensor_tensor(d3, d3, t3, ALU.add), c, d)

    def ev_q(i):
        def ev(full, t):
            a, r = rope(fv(Q2 + 1024 * i, 1024), full, 4, t)
            done["Q%d" % i] = r
            return [a]
        return ev

    def ev_kv(full, t):
        kt_ = fv(VT + 512, 512)
        a, r = rope(kt_, full[:, 0:512], 2, t, gT["x"])
        for j in range(4):
            src = kt_[64 * (j % 2):64 * (j % 2) + 64, (j // 2) * T:(j // 2) * T + T]
            for half in range(2):
                c = dve.do(lambda e, j=j, half=half, src=src: e.tensor_copy(F[64 * half:64 * half + 64, KK + j * T:KK + j * T + T], src), r)
        done["K"] = c
        a2 = act.do(lambda e: e.copy(fv(VT, 512), full[:, 512:1024]), t)
        for m in range(2):
            for i in range(2):
                b = pe.do(lambda e, m=m, i=i: e.transpose(PS[:, 6, i * T + m * P:i * T + m * P + P],
                                                          fv(VT + m * T + i * P, P), ident[:, :]), a2, mfree[6])
        v = act.do(lambda e: e.copy(fv(VN, 512), PS[:, 6, :]), b)
        mfree[6] = [v]
        done["V"] = v
        return [a2]

    for i in range(4):
        panel(win2, 0, 16, 4096 + i * 512, H, ev_q(i))
    panel(win2, 0, 16, 6144, H, ev_kv)

    aw2 = F[:, 17408:17408 + 2 * 1600].rearrange("p (r n) -> p r n", r=2)
    af2 = [None, None]

    def head2(pr, r):
        kv = pr // 4
        w = aw2[:, r, :]
        s_ = w[:, 0:768]
        pt = w[:, 768:1536]
        mx, sm, es_ = w[:, 1536:1540], w[:, 1540:1544], w[:, 1544:1548]
        ba = (4, 5) if r == 0 else (6, 7)
        qt = Q2 + pr * T
        tq = [done["Q%d" % (pr // 4)], done["K"]]
        for x in range(2):
            hs = slice(64 * x, 64 * x + 64)
            pe.do(lambda e, x=x, hs=hs: e.matmul(PS[:, ba[x], 0:256], F[hs, qt + 128:qt + 256], F[hs, KK + kv * T:KK + kv * T + T],
                                                 start=True, stop=True), tq, mfree[ba[x]])
            p1 = pe.do(lambda e, x=x, hs=hs: e.matmul(PS[:, ba[x], 256:384], F[hs, qt:qt + 128], F[hs, KK + kv * T:KK + kv * T + P],
                                                      start=True, stop=True))
        yield
        for x in range(2):
            o = x * 384
            d1 = dve.do(lambda e, x=x, o=o: e.scalar_tensor_tensor(s_[:, o:o + 256], PS[:, ba[x], 0:256], 0.125, msk, ALU.mult, ALU.add), p1, af2[r])
            d1 = dve.do(lambda e, x=x, o=o: e.scalar_tensor_tensor(s_[:, o + 256:o + 384], PS[:, ba[x], 256:384], 0.125, msk[:, 128:256], ALU.mult, ALU.add))
        for x in range(2):
            o = x * 384
            dve.do(lambda e, x=x, o=o: e.tensor_reduce(mx[:, 2 * x:2 * x + 1], s_[:, o:o + 256], AX, ALU.max), d1)
            d2 = dve.do(lambda e, x=x, o=o: e.tensor_reduce(mx[:, 2 * x + 1:2 * x + 2], s_[:, o + 256:o + 384], AX, ALU.max))
        skb = sink[:, 2 * pr:2 * pr + 2].unsqueeze(2).broadcast_to([P, 2, 2])
        v2 = lambda v: v.rearrange("p (a b) -> p a b", a=2)
        d3 = dve.do(lambda e: e.tensor_tensor(v2(mx), v2(mx), skb, ALU.max), d2)
        d4 = dve.do(lambda e: e.tensor_tensor(v2(es_), skb, v2(mx), ALU.subtract), d3)
        d5 = dve.do(lambda e: e.tensor_scalar(mx, mx, -1.0, None, ALU.mult), d4)
        a0 = act.do(lambda e: e.activation(es_, es_, ACT.Exp), d4)
        for x in range(2):
            o = x * 384
            act.do(lambda e, x=x, o=o: e.activation(s_[:, o:o + 256], s_[:, o:o + 256], ACT.Exp, bias=mx[:, 2 * x:2 * x + 1], accum_out=sm[:, 2 * x:2 * x + 1]), d5)
            a1 = act.do(lambda e, x=x, o=o: e.activation(s_[:, o + 256:o + 384], s_[:, o + 256:o + 384], ACT.Exp, bias=mx[:, 2 * x + 1:2 * x + 2], accum_out=sm[:, 2 * x + 1:2 * x + 2]))
        yield
        d6 = dve.do(lambda e: e.tensor_tensor(sm, sm, es_, ALU.add), a1)
        d7 = dve.do(lambda e: e.reciprocal(sm, sm), d6)
        for x in range(2):
            o = x * 384
            dve.do(lambda e, x=x, o=o: e.tensor_scalar(s_[:, o:o + 256], s_[:, o:o + 256], sm[:, 2 * x:2 * x + 1], None, ALU.mult), d7)
            d8 = dve.do(lambda e, x=x, o=o: e.tensor_scalar(s_[:, o + 256:o + 384], s_[:, o + 256:o + 384], sm[:, 2 * x + 1:2 * x + 2], None, ALU.mult))
        yield
        for x in range(2):
            o = x * 384
            for src, dst in ((256, 0), (0, 128), (128, 256)):
                p3 = pe.do(lambda e, x=x, o=o, src=src, dst=dst: e.transpose(PS[:, ba[x], dst:dst + P], s_[:, o + src:o + src + P], ident[:, :]), d8)
        yield
        for x in range(2):
            a3 = act.do(lambda e, x=x: e.copy(pt[:, x * 384:x * 384 + 384], PS[:, ba[x], 0:384]), p3)
        yield
        for x in range(2):
            hs = slice(64 * x, 64 * x + 64)
            o = x * 384
            pe.do(lambda e, hs=hs, o=o: e.matmul(PS[hs, ba[0], 0:256], fv(VN + kv * 64, 64), pt[:, o:o + 256], start=True, stop=False,
                                                 skip_group_check=True), a3, done["V"])
            p4 = pe.do(lambda e, hs=hs, o=o: e.matmul(PS[hs, ba[0], 128:256], fv(VN + 256 + kv * 64, 64), pt[:, o + 256:o + 384],
                                                      start=False, stop=True, skip_group_check=True))
        af2[r] = p4
        yield
        t = act.do(lambda e: e.copy(fv(qt, 256), PS[:, ba[0], 0:256]), p4)
        mfree[ba[0]] = [t]
        mfree[ba[1]] = [t]
        done["O%d" % pr] = t

    def attn2_task():
        for pair in range(8):
            g = [head2(2 * pair, 0), head2(2 * pair + 1, 1)]
            while g:
                for x in list(g):
                    try:
                        next(x)
                    except StopIteration:
                        g.remove(x)
                yield

    call(lambda: background.append(attn2_task()))
    G1 = 0
    G2 = None
    gate_at = {}
    def wait_scan():
        waitfor["gr0"] = [yt["x"]]

    call(wait_scan)
    for i in range(4):
        panel(win2, 0, 16, 6656 + i * 512, H, ev_tanh(fv(i * 1024, 1024), "gr%d" % i), bg=2)

    def heads_done():
        while background:
            step()
        waitfor["gt0"] = [(pe.sem, pe.n), (dve.sem, dve.n), (act.sem, act.n)]

    GT = 14336
    for i in range(4):
        if i == 0:
            call(heads_done)
        panel(win2, 0, 16, 8704 + i * 512, H, ev_tanh(fv(GT + i * 1024, 1024), "gt%d" % i), bg=2)

    def convert_att():
        tf = (pe.sem, pe.n)
        def task():
            for i in range(4):
                split_out(YA, 4 * i, 4, fv(Q2 + 1024 * i, 1024), 1.0, done["O%d" % (4 * i + 3)], tf)
                yield
        background.append(task())

    call(convert_att)
    wrp, wap = w2("w_rnn_proj_2"), w2("w_attn_proj_2")
    for i in range(4):
        panel(wrp, 0, 16, i * 512, xc, ev_gate1(i * 1024, "rp%d" % i))
    mgf = [None]

    def att_ready():
        while background:
            step()
        mgf[0] = (pe.sem, pe.n)

    call(att_ready)
    for i in range(4):
        panel(wap, 0, 16, i * 512, YA, ev_gate2(GT + i * 1024, i * 1024, MG, 4 * i, "ap%d" % i, lambda: [mgf[0]]))
    O = 4096
    O3 = f3(O, 16)
    wo2 = w2("w_out_2")

    def ev_o(p, ch, last):
        def ev(full, t):
            o = fv(O + 1024 * p, 1024)
            if ch == 0:
                r = dve.do(lambda e: e.tensor_copy(o, full), t, onorm[0])
            else:
                r = dve.do(lambda e: e.tensor_tensor(o, o, full, ALU.add), t, onorm[0])
            if last:
                add_squares(o, p, r)
            return [r]
        return ev

    onorm = [None]

    def before_o():
        onorm[0] = [(act.sem, act.n), (dve.sem, dve.n)]

    call(before_o)
    for i in range(4):
        panel(wo2, 0, 16, i * 512, MG, ev_o(i, 0, True))

    def norm4():
        ts = stats(4, ssf["t"], mfree[4])
        ssf["use"] = ts
        gp = cols[:, C_POST:C_POST + 16]
        for p in range(4):
            for k in range(4 * p, 4 * p + 4):
                r = dve.do(lambda e, k=k: e.scalar_tensor_tensor(O3[:, k, :], O3[:, k, :], gp[:, k:k + 1], rstd[:, :], ALU.mult, ALU.mult), ts)
            r = dve.do(lambda e, p=p: e.tensor_tensor(fv(XR + 1024 * p, 1024), fv(XR + 1024 * p, 1024), fv(O + 1024 * p, 1024), ALU.add), r)
            add_squares(fv(XR + 1024 * p, 1024), p, r)
        ts = stats(4, ssf["t"], r)
        ssf["use"] = ts
        apply_norm(xr3, cols[:, C_MPRE:C_MPRE + 16], None, H2, ts, (pe.sem, pe.n))
        onorm[0] = [(dve.sem, dve.n)]
        fff[0] = fff[1] = (dve.sem, dve.n)

    call(norm4)
    ffn(w2("w_mlp_up_2"), w2("w_mlp_down_2"), H2, HID, lambda ch, i: ev_o(i, ch, ch == 3), "2")

    def finale():
        ts = stats(4, ssf["t"], mfree[4])
        gp = cols[:, C_MPOST:C_MPOST + 16]
        yo = F[:, 14336:14336 + 4096].rearrange("p (i n) -> p i n", i=2)
        toks = []
        fr_ = [None, None]
        for p in range(8):
            for k in range(2 * p, 2 * p + 2):
                r = dve.do(lambda e, k=k: e.scalar_tensor_tensor(O3[:, k, :], O3[:, k, :], gp[:, k:k + 1], rstd[:, :], ALU.mult, ALU.mult), ts)
            r = dve.do(lambda e, p=p: e.tensor_tensor(fv(XR + 512 * p, 512), fv(XR + 512 * p, 512), fv(O + 512 * p, 512), ALU.add), r)
            bank = 4 + p % 4
            for i in range(2):
                for j in range(2):
                    k = 2 * p + j
                    tt = pe.do(lambda e, i=i, j=j, k=k, bank=bank: e.transpose(
                        PS[:, bank, i * T + j * P:i * T + j * P + P], xr3[:, k, i * P:i * P + P], ident[:, :]),
                        r, toks[p - 4] if p >= 4 else ts)
            toks.append(act.do(lambda e, p=p, bank=bank: e.copy(yo[:, :, 2 * p * P:2 * p * P + 256],
                                                                PS[:, bank, :].rearrange("p (i n) -> p i n", i=2)), tt, ts))
            if p % 4 == 3:
                c0 = (p // 4) * 1024
                fin.append(dma(sp, [(out[0, i * P:(i + 1) * P, c0:c0 + 1024], yo[:, i, c0:c0 + 1024]) for i in range(2)], toks[-1]))
        sp.wait(*fin)
        sp.wait(t_xs, t_bs)

    fin = []
    call(finale)

    ada_groups = [(2, 0), (2, 1), (3, 0), (3, 1), (4, 0), (4, 1), (5, 0), (5, 1)]
    spread = {}
    flat = [u for u in units]
    first = flat[:64]
    rest = flat[64:]
    order = list(first)
    extra = []
    for g, q in ada_groups:
        for kt, (src, use) in enumerate(add_ada_group(g, q)):
            extra.append({"kind": "ada", "src": src, "nk": 1, "use": use, "close": (g, q) if kt == 15 else None})
    for n, u in enumerate(rest):
        order.append(u)
        due = min(96, 1 + n // 2) if n < 200 else min(128, 96 + n - 199)
        while extra and 128 - len(extra) < due:
            order.append(extra.pop(0))
    assert not extra
    units[:] = order
    for j, u in enumerate(units):
        index_of[id(u)] = j
    for j in range(RAWN):
        send(j)
    for item in runs:
        if isinstance(item, Panel):
            run_panel(item)
        else:
            item()


_OUT = (1, 256, 2048)


def kernel(**inputs):
    import concourse.bacc as bacc
    from concourse.bass_utils import run_bass_kernel_spmd

    nc = bacc.Bacc("TRN2", target_bir_lowering=False, num_devices=1)
    arrays, aps = {}, {}
    for name, a in list(inputs.items()) + list(constants().items()):
        a = np.ascontiguousarray(a)
        arrays["in_" + name] = a
        aps[name] = nc.dram_tensor("in_" + name, a.shape, mybir.dt.from_np(a.dtype), kind="ExternalInput").ap()
    out = nc.dram_tensor("out_0", _OUT, F32, kind="ExternalOutput").ap()
    scr_x = nc.dram_tensor("scr_x", (P, 4096), F32, kind="Internal").ap()
    scr_b = nc.dram_tensor("scr_b", (8, 384), F32, kind="Internal").ap()
    build(nc, aps, out, scr_x, scr_b)
    r = run_bass_kernel_spmd(nc, [arrays], core_ids=[0])
    return r.results[0]["out_0"]
```

```python
from contextlib import ExitStack
import math

import numpy as np
import concourse.bass as bass
from concourse import mybir
from concourse.alu_op_type import AluOpType as ALU

F32 = mybir.dt.float32
F32R = mybir.dt.float32r
I32 = mybir.dt.int32
ACT = mybir.ActivationFunctionType
AX = mybir.AxisListType.X

P = 128
T = 256
D = 2048
NEG = -1e30
RAWN = 4
SPN = 4
LOOK = 3
ADAP = ((8, 0), (80, 40), (128, 76), (136, 78), (168, 86), (192, 104), (232, 128))
MAGIC = 12582912.0
TWO_PI = 2.0 * math.pi
GELU_C = 0.7978845608028654
GELU_A = 0.044715


def two_pi_parts():
    c1 = np.float32(6.28125)
    c2 = np.float32(np.round((TWO_PI - float(c1)) * 2.0 ** 21) / 2.0 ** 21)
    c3 = np.float32(TWO_PI - float(c1) - float(c2))
    return float(c1), float(c2), float(c3)


def bucket_of(n):
    if n < 16:
        return n
    v = np.log(np.float32(n) / np.float32(16)) / np.float32(math.log(128 / 16)) * np.float32(16)
    return min(16 + int(np.float32(v)), 31)


def constants():
    ident = np.eye(P, dtype=np.float32)
    hot = np.zeros((32, 384), np.float32)
    neg = np.zeros((8, 384), np.float32)
    for j in range(384):
        rel = 255 - j
        if rel >= 0:
            hot[bucket_of(rel), j] = 1.0
        else:
            neg[:, j] = NEG
    inv = np.float32(10000.0) ** (-np.arange(0, 64, 2, dtype=np.float32) / np.float32(64))
    part = np.zeros((P, 4), np.float32)
    part[:, 0] = np.tile(inv.astype(np.float32), 4)
    par = (np.arange(P) // 16) % 2
    part[:, 1] = (par == 0)
    part[:, 2] = (par == 1)
    swap = np.zeros((P, P), np.float32)
    for m in range(P):
        b, r = m // 64 * 64, m % 64
        if r < 32:
            swap[b + r + 32, m] = -1.0
        else:
            swap[b + r - 32, m] = 1.0
    q, k = np.arange(P)[:, None], np.arange(P)[None, :]
    mask = np.concatenate([np.where(k > q, 0.0, NEG), np.where(k <= q, 0.0, NEG)], 1).astype(np.float32)
    swap = np.concatenate([swap, ident[::-1]], 1)
    return {"c_ident": ident, "c_hot": hot, "c_neg": neg, "c_part": part, "c_swap": swap, "c_mask": mask}


class Engine:

    def __init__(self, e, sem):
        self.e, self.sem, self.n, self.seen = e, sem, 0, {}

    def wait(self, *tokens):
        for t in tokens:
            if t is None:
                continue
            if isinstance(t, list):
                self.wait(*t)
                continue
            sem, v = t
            if self.seen.get(id(sem), 0) < v:
                self.seen[id(sem)] = v
                self.e.wait_ge(sem, v)

    def do(self, f, *tokens):
        self.wait(*tokens)
        self.n += 1
        f(self.e).then_inc(self.sem, 1)
        return (self.sem, self.n)

    def quiet(self, f, *tokens):
        self.wait(*tokens)
        f(self.e)


def build(nc, I, out, scr_x, scr_b):
    with ExitStack() as ctx:
        _build(nc, ctx, I, out, scr_x, scr_b)


def _build(nc, ctx, I, out, scr_x, scr_b):
    def sb(name, shape, dt=F32):
        return ctx.enter_context(nc.sbuf_tensor(name, shape, dt))

    def sem(name):
        return ctx.enter_context(nc.semaphore(name))

    raw = sb("raw", [P, RAWN, 1024])
    whi = sb("whi", [P, SPN, 1024], F32R)
    wlo = sb("wlo", [P, SPN, 1024], F32R)
    R = sb("R", [P, 16384], F32R)
    F = sb("F", [P, 21504])
    ident = sb("ident", [P, P])
    ones = sb("ones", [P, P])
    cols = sb("cols", [P, 480])
    mod = sb("mod", [P, 96])
    der = sb("der", [P, 16, 16])
    PS = ctx.enter_context(nc.psum_tensor("PS", [P, 8, 512], F32))

    pe = Engine(nc.tensor, sem("s_pe"))
    act = Engine(nc.scalar, sem("s_act"))
    dve = Engine(nc.vector, sem("s_dve"))
    pool = Engine(nc.gpsimd, sem("s_pool"))
    sp = Engine(nc.sync, sem("s_sp"))
    raw_sem = [sem(f"s_raw{i}") for i in range(RAWN)]
    nsem = [0]

    def dma(eng, pairs, *tokens):
        s = sem(f"s_dma{nsem[0]}")
        nsem[0] += 1
        eng.wait(*tokens)
        for o, i in pairs:
            eng.e.dma_start(o, i).then_inc(s, 16)
        return (s, 16 * len(pairs))

    def fv(off, n):
        return F[:, off:off + n]

    def f3(off, k, n=T):
        return F[:, off:off + k * n].rearrange("p (k n) -> p k n", k=k)

    class Operand:

        def __init__(self, *blocks):
            self.b = blocks
            self.ready = [None] * (8 * len(blocks))

        def hi(self, k, n=1):
            o = self.b[k // 8] * 4096 + (k % 8) * T
            return R[:, o:o + n * T]

        def lo(self, k, n=1):
            o = self.b[k // 8] * 4096 + 2048 + (k % 8) * T
            return R[:, o:o + n * T]

    def hi_out(op, k, n, src, scale, *tokens):
        return act.do(lambda e: e.activation(op.hi(k, n), src, ACT.Copy, scale=scale), *tokens)

    def lo_out(op, k, n, src, scale, a):
        if scale == 1.0:
            b = dve.do(lambda e: e.tensor_tensor(op.lo(k, n), src, op.hi(k, n).bitcast(F32), ALU.subtract), a)
        else:
            b = dve.do(lambda e: e.scalar_tensor_tensor(op.lo(k, n), src, scale, op.hi(k, n).bitcast(F32),
                                                        ALU.mult, ALU.subtract), a)
        for j in range(k, k + n):
            op.ready[j] = b
        return b

    def split_out(op, k, n, src, scale, *tokens):
        return lo_out(op, k, n, src, scale, hi_out(op, k, n, src, scale, *tokens))

    units = []
    state = {"prep": 0, "w": 0, "sent": 0}
    released = {}
    used = {}

    def send(j):
        u = units[j]
        s = j % RAWN
        toks = released[j - RAWN] if j >= RAWN else []
        sp.wait(*toks)
        dst = raw[:, s, :].rearrange("p (k n) -> p k n", k=u["nk"])
        src = u["src"]
        sp.e.dma_start(dst, src).then_inc(raw_sem[s], 16)

    def landed(j):
        return (raw_sem[j % RAWN], 16 * (j // RAWN + 1))

    def prep(j):
        u = units[j]
        r = raw[:, j % RAWN, :]
        if u["kind"] == "w":
            w = state["w"]
            state["w"] += 1
            u["w"] = w
            s = w % SPN
            free = used.get(w - SPN)
            a = act.do(lambda e: e.activation(whi[:, s, :], r, ACT.Copy), landed(j), free)
            b = dve.do(lambda e: e.tensor_tensor(wlo[:, s, :], r, whi[:, s, :].bitcast(F32), ALU.subtract),
                       landed(j), a, free)
            u["ready"] = [a, b]
            released[j] = [a, b]
        else:
            released[j] = [u["use"](r, landed(j))]
        if j + RAWN < len(units):
            send(j + RAWN)

    def advance(to):
        to = min(to, len(units) - 1)
        while state["prep"] <= to:
            prep(state["prep"])
            state["prep"] += 1

    gbuf = [0]
    gfree = [None, None]

    class Panel:
        pass

    panels = []

    def add_panel(srcs, nk, mms, operand, evac):
        p = Panel()
        p.units = []
        for s in srcs:
            u = {"kind": "w", "src": s, "nk": nk}
            p.units.append(u)
            units.append(u)
        p.mms, p.operand, p.evac = mms, operand, evac
        panels.append(p)
        return p

    def add_ada(src, use):
        units.append({"kind": "ada", "src": src, "nk": 1, "use": use})

    background = []

    def step():
        for g in list(background):
            if next(g, "end") == "end":
                background.remove(g)

    def drain(*names):
        while background and (not names or any(x not in done for x in names)):
            step()

    index_of = {}
    ahead = {}

    def evacuate(ev, b):
        for t in ev:
            if t is not None and gfree[b] == "busy":
                gfree[b] = [t]
            yield

    def run_panel(p):
        b = gbuf[0] % 2
        gbuf[0] += 1
        while gfree[b] == "busy":
            step()
        pe.wait(gfree[b])
        seen_bank = set()
        last = len(p.units) - 1
        for n, u in enumerate(p.units):
            j = index_of[id(u)]
            advance(j)
            pe.wait(*u["ready"])
            s = u["w"] % SPN
            todo = p.mms(n)
            for col, k, m in todo:
                while p.operand.ready[k] is None:
                    step()
                pe.wait(p.operand.ready[k])
                o = PS[:, 2 * b + m // 2, (m % 2) * T:(m % 2) * T + T]
                bank = m // 2
                for a, (w, x) in enumerate(((whi, p.operand.hi(k)), (whi, p.operand.lo(k)), (wlo, p.operand.hi(k)))):
                    first = bank not in seen_bank
                    seen_bank.add(bank)
                    stop = n == last and a == 2 and (col, k, m) == [t for t in todo if t[2] == m][-1]
                    fn = lambda e, o=o, w=w, x=x, first=first, stop=stop, col=col, s=s: e.matmul(
                        o, w[:, s, col:col + P], x, start=first, stop=stop, skip_group_check=True)
                    if a == 2 and (col, k, m) == todo[-1]:
                        tok = pe.do(fn)
                    else:
                        pe.quiet(fn)
            used[u["w"]] = tok
            advance(ahead[j])
            if n < last:
                step()
        full = PS[:, 2 * b:2 * b + 2, :].rearrange("p a n -> p (a n)")
        ev = p.evac(full, tok)
        gfree[b] = "busy"
        task = evacuate(ev, b)
        if next(task, "end") != "end":
            background.append(task)
        step()

    def std(W, k0, nkt, c0):
        v = W.rearrange("(k p) n -> p k n", p=P)
        srcs = [v[:, k0 + 2 * u:k0 + 2 * u + 2, c0:c0 + 512] for u in range(nkt // 2)]
        mms = lambda u: [(kk * 512 + m * P, 2 * u + kk, m) for kk in range(2) for m in range(4)]
        return srcs, mms

    GT1 = 14336
    GA, GB = 0, 4096
    U = 8192
    E0 = 10240
    SW = 14336
    LB = 17408
    CT = 19456
    XN = 17408
    Q, K, V = 10240, 12288, 14336
    BH = 16384
    AW = 18432
    X = 0
    STG = 12288
    XT = 0
    w2 = lambda n: I[n].rearrange("o a b -> (o a) b")
    rows = lambda n: I[n].rearrange("o (k p) -> (o k) p", p=P)
    S0, S1, S2, S3 = (fv(STG + 128 * i, 128) for i in range(4))
    small = [
        (ident[:, :], I["c_ident"]),
        (S0[0:16, :], rows("c")), (S0[16:32, :], rows("norm_mix_g")), (S0[32:128, :], rows("b_ada")),
        (S1[0:16, :], rows("norm_mlp_g")), (S1[16:32, :], I["norm_final_g"].rearrange("(k p) -> k p", p=P)),
        (S1[32:40, :], rows("ssm_d")), (S1[40:48, :], rows("b_glu")),
        (S1[48:64, :], rows("norm_mix_pre_2")), (S1[64:80, :], rows("norm_mix_post_2")),
        (S1[80:96, :], rows("norm_mlp_pre_2")), (S1[96:112, :], rows("norm_mlp_post_2")),
        (S1[112:128, :], rows("lru_lambda_2")),
        (S2[0:64, :], I["conv_w_2"].rearrange("o w (k p) -> (o w k) p", p=P)),
        (S2[64:80, :], rows("conv_b_2")), (S2[80:96, :], rows("b_rg_a_2")), (S2[96:112, :], rows("b_rg_x_2")),
        (S3[0:32, :], I["ssm_a_re"].rearrange("o (t s) n -> (o t) (s n)", s=2)),
        (S3[32:64, :], I["ssm_a_im"].rearrange("o (t s) n -> (o t) (s n)", s=2)),
    ]
    ldt = fv(STG + 512, 2)
    small.append((ldt[64:96, :], I["ssm_log_dt"].rearrange("o (t s) -> (o t) s", s=2)))
    t_small = dma(act, small)
    xn = f3(XN, 2, D)
    t_x = dma(act, [(xn[:, i, :], I["x"][0, i * P:(i + 1) * P, :]) for i in range(2)])
    relb = fv(STG + 516, 8)
    hot = fv(STG + 524, 384)
    negr = fv(STG + 908, 384)
    part = sb("part", [P, 4])
    t_hot = dma(act, [(relb[0:32, :], I["rel_bias"]), (hot[0:32, :], I["c_hot"]), (negr[0:8, :], I["c_neg"]),
                      (part[:, :], I["c_part"])])
    BB = 14336
    bsr = f3(BB, 2, 512)
    csr = f3(BB + 1024, 2, 512)
    t_bc = dma(act, [
        (bsr[:, 0, :].rearrange("q (t p) -> q t p", t=32), I["ssm_b_re"].rearrange("o (t s) n p -> (o s n) t p", s=2)),
        (bsr[:, 1, :].rearrange("q (t p) -> q t p", t=32), I["ssm_b_im"].rearrange("o (t s) n p -> (o s n) t p", s=2)),
        (csr[:, 0, :].rearrange("q (f n) -> q f n", f=8), I["ssm_c_re"].rearrange("o (f g) p n -> (o g p) f n", g=8)),
        (csr[:, 1, :].rearrange("q (f n) -> q f n", f=8), I["ssm_c_im"].rearrange("o (f g) p n -> (o g p) f n", g=8)),
    ])
    C_C, C_G1, C_BADA = 0, 16, 32
    C_GM, C_GF, C_SD, C_BG = 128, 144, 160, 168
    C_PRE, C_POST, C_MPRE, C_MPOST, C_LAM = 176, 192, 208, 224, 240
    C_CW, C_CB, C_BA, C_BX = 256, 320, 336, 352
    C_AR, C_AI, C_LD = 384, 416, 448

    dcol = lambda i, n=16: der[:, i, 0:n]
    cact, A1, A2, hbg, spc, hba, hbx, eps = (dcol(i) for i in range(8))

    t_one = dve.do(lambda e: e.memset(ones[:, :], 1.0))
    t_eps = dve.do(lambda e: e.memset(eps, 1e-6))
    eps2 = dcol(14, 1)
    t_e2 = dve.do(lambda e: e.memset(eps2, 1e-12))
    t = dve.do(lambda e: e.tensor_copy(S3[64:96, :].rearrange("p (s n) -> p s n", s=2),
                                       ldt[64:96, :].unsqueeze(2).broadcast_to([32, 2, 64])), t_small)
    for i, (S, n) in enumerate(((S0, 128), (S1, 128), (S2, 112), (S3, 96))):
        tt = pe.do(lambda e, S=S, n=n, i=i: e.transpose(PS[:, 4, i * 128:i * 128 + n], S[0:n, :], ident[0:n, 0:n]), t_small, t)
    t_cols = [act.do(lambda e, n=n, i=i: e.copy(cols[:, i * 128:i * 128 + n], PS[:, 4, i * 128:i * 128 + n]), tt)
              for i, n in enumerate((128, 128, 112, 96))]
    c = cols[:, C_C:C_C + 16]
    th = dcol(8)
    ta = act.do(lambda e: e.activation(th, c, ACT.Tanh, scale=0.5), t_cols[0])
    tb = dve.do(lambda e: e.scalar_tensor_tensor(cact, th, 1.0, c, ALU.add, ALU.mult), ta)
    t_c = dve.do(lambda e: e.tensor_scalar(cact, cact, 0.5, None, ALU.mult), tb)
    tk = t_cols[1]

    pw = sb("pw", [P, 12, 32])
    pv = lambda i: pw[:, i, :]
    are, aim = cols[:, C_AR:C_AR + 32], cols[:, C_AI:C_AI + 32]
    mag, ec, es, fr, fi = pv(0), pv(1), pv(2), pv(3), pv(4)
    dt_, th_, a_, b_, c_, d_, g_ = (pv(i) for i in range(5, 12))
    C1, C2, C3 = two_pi_parts()

    def reduce_angle(v, k, t):
        t = dve.do(lambda e: e.tensor_scalar(k, v, 1.0 / TWO_PI, MAGIC, ALU.mult, ALU.add), t)
        t = dve.do(lambda e: e.tensor_scalar(k, k, -MAGIC, None, ALU.add), t)
        for cc in (C1, C2, C3):
            t = dve.do(lambda e: e.scalar_tensor_tensor(v, k, -cc, v, ALU.mult, ALU.add), t)
        return dve.do(lambda e: e.tensor_scalar(v, v, 3.1415925, -3.1415925, ALU.min, ALU.max), t)

    def sincos(v, co, si, t):
        t = act.do(lambda e: e.activation(si, v, ACT.Sin), t)
        t2 = act.do(lambda e: e.activation(co, v, ACT.Sin, scale=0.5), t)
        t3 = dve.do(lambda e: e.tensor_tensor(co, co, co, ALU.mult), t2)
        return dve.do(lambda e: e.tensor_scalar(co, co, -2.0, 1.0, ALU.mult, ALU.add), t3)

    t0 = act.do(lambda e: e.activation(dt_, cols[:, C_LD:C_LD + 32], ACT.Exp), t_cols[3])
    t1 = dve.do(lambda e: e.tensor_tensor(a_, dt_, are, ALU.mult), t0)
    t_mag = act.do(lambda e: e.activation(mag, a_, ACT.Exp), t1)
    t1 = dve.do(lambda e: e.tensor_tensor(th_, dt_, aim, ALU.mult), t1)
    t1 = reduce_angle(th_, b_, t1)
    t_e = sincos(th_, ec, es, t1)
    ss = sb("ss", [P, T])
    rstd = sb("rstd", [P, T])
    tx = []
    t_sq, t_ss, t_xs, t_f, t_sp = [None], [None], [None], [None], [None]
    mfree = {4: None, 5: None, 6: None, 7: None}

    def x_task():
        for f2 in range(8):
            bank = 4 + f2 % 3
            for i in range(2):
                for j in range(2):
                    kt = 2 * f2 + j
                    tt = pe.do(lambda e: e.transpose(PS[:, bank, j * T + i * P:j * T + i * P + P], xn[:, i, kt * P:(kt + 1) * P],
                                                     ident[:, :]), t_x, t_small, t_cols[-1], mfree[5], tx[f2 - 3] if f2 >= 3 else None)
            tx.append(act.do(lambda e: e.copy(fv(XT + f2 * 512, 512), PS[:, bank, :]), tt))
            if f2 % 2:
                yield
        for b in (4, 5, 6):
            mfree[b] = [tx[-1]]
        t_xs[0] = dma(pool, [(scr_x, fv(XT, 4096))], tx[-1])
        sq = fv(9216, 1024)
        part_ = fv(16384, 256)
        t = None
        for p in range(4):
            a = act.do(lambda e: e.activation(sq, fv(XT + p * 1024, 1024), ACT.Square), t, tx[-1])
            yield
            v = sq.rearrange("p (k n) -> p n k", k=4)
            if p == 0:
                t = dve.do(lambda e: e.tensor_reduce(ss[:, :], v, AX, ALU.add), a)
            else:
                t = dve.do(lambda e: e.tensor_reduce(part_, v, AX, ALU.add), a)
                t = dve.do(lambda e: e.tensor_tensor(ss[:, :], ss[:, :], part_, ALU.add), t)
            yield
        t_ss[0] = stats(4, t, mfree[4])
        mfree[4] = [t_ss[0]]

    def param_task():
        t1 = dve.do(lambda e: e.tensor_tensor(a_, mag, ec, ALU.mult), t_e, t_mag)
        t1 = dve.do(lambda e: e.tensor_scalar(a_, a_, -1.0, None, ALU.add), t1)
        t2 = dve.do(lambda e: e.tensor_tensor(b_, mag, es, ALU.mult), t1)
        dve.do(lambda e: e.tensor_tensor(c_, are, are, ALU.mult))
        t4 = dve.do(lambda e: e.tensor_tensor(d_, aim, aim, ALU.mult))
        t3 = dve.do(lambda e: e.tensor_tensor(c_, c_, d_, ALU.add), t4)
        yield
        t3 = dve.do(lambda e: e.reciprocal(c_, c_), t3)
        t4 = dve.do(lambda e: e.tensor_tensor(d_, a_, are, ALU.mult), t3)
        t5 = dve.do(lambda e: e.tensor_tensor(g_, b_, aim, ALU.mult), t4)
        t5 = dve.do(lambda e: e.tensor_tensor(d_, d_, g_, ALU.add), t5)
        t5 = dve.do(lambda e: e.tensor_tensor(fr, d_, c_, ALU.mult), t5)
        yield
        t6 = dve.do(lambda e: e.tensor_tensor(d_, b_, are, ALU.mult), t5)
        t6 = dve.do(lambda e: e.tensor_tensor(g_, a_, aim, ALU.mult), t6)
        t6 = dve.do(lambda e: e.tensor_tensor(d_, d_, g_, ALU.subtract), t6)
        t_f[0] = dve.do(lambda e: e.tensor_tensor(fi, d_, c_, ALU.mult), t6)
        yield
        dve.do(lambda e: e.tensor_scalar(dcol(3, 8), cols[:, C_BG:C_BG + 8], 0.5, None, ALU.mult), tk)
        dve.do(lambda e: e.tensor_scalar(hba, cols[:, C_BA:C_BA + 16], 0.5, None, ALU.mult), t_cols[2])
        dve.do(lambda e: e.tensor_scalar(hbx, cols[:, C_BX:C_BX + 16], 0.5, None, ALU.mult))
        lam = cols[:, C_LAM:C_LAM + 16]
        s9, s10, z, z2, q = (dcol(i) for i in range(9, 14))
        t1 = dve.do(lambda e: e.tensor_scalar(s9, lam, -1.0, None, ALU.mult))
        t1 = dve.do(lambda e: e.tensor_tensor(s10, s9, lam, ALU.min), t1)
        t2 = act.do(lambda e: e.activation(s10, s10, ACT.Exp), t1)
        yield
        t1 = dve.do(lambda e: e.tensor_scalar(z, s10, 2.0, None, ALU.add), t2)
        t1 = dve.do(lambda e: e.reciprocal(z, z), t1)
        t1 = dve.do(lambda e: e.tensor_tensor(z, z, s10, ALU.mult), t1)
        t1 = dve.do(lambda e: e.tensor_tensor(z2, z, z, ALU.mult), t1)
        t1 = dve.do(lambda e: e.tensor_scalar(q, z2, 1.0 / 17, None, ALU.mult), t1)
        yield
        for n in (15, 13, 11, 9, 7, 5, 3):
            t1 = dve.do(lambda e: e.scalar_tensor_tensor(q, q, 1.0 / n, z2, ALU.add, ALU.mult), t1)
        t1 = dve.do(lambda e: e.scalar_tensor_tensor(q, q, 1.0, z, ALU.add, ALU.mult), t1)
        t1 = dve.do(lambda e: e.tensor_scalar(s9, s9, 0.0, None, ALU.max), t1)
        t1 = dve.do(lambda e: e.scalar_tensor_tensor(s9, q, 2.0, s9, ALU.mult, ALU.add), t1)
        t_sp[0] = dve.do(lambda e: e.tensor_scalar(spc, s9, -4.0, None, ALU.mult), t1)

    def stats(bank, *tokens):
        t = pe.do(lambda e: e.matmul(PS[:, bank, 0:T], ones[:, :], ss[:, :], start=True, stop=True), t_one, *tokens)
        t = act.do(lambda e: e.activation(rstd[:, :], PS[:, bank, 0:T], ACT.Sqrt, scale=1.0 / D, bias=eps[:, 0:1]), t, t_eps)
        return dve.do(lambda e: e.reciprocal(rstd[:, :], rstd[:, :]), t)

    lb = F[:, LB:LB + 2048].rearrange("p (c f s) -> p c f s", c=2, f=8)
    ct = F[:, CT:CT + 2048].rearrange("p (c f s) -> p c f s", c=2, f=8)
    t_lc = []

    def matrix_task():
        xh = F[:, 15360:16384].rearrange("p (t s q) -> p t s q", t=32, s=2)
        xh2 = F[:, 15360:16384].rearrange("p (f s) -> p f s", f=8)
        m_ = fv(9216, 1024).rearrange("p (c t q) -> p c t q", c=2, t=32)
        bc = lambda v: v.unsqueeze(2).broadcast_to([P, 32, 16])
        bre, bim = (bsr[:, i, :].rearrange("p (t q) -> p t q", t=32) for i in range(2))
        tfree = [tx[-1], t_ss[0]]
        prev = None
        xc_ = F[:, CT:CT + 2048].rearrange("p (c f s n) -> p c f s n", c=2, f=8, s=2)
        for ci in range(2):
            for h in range(2):
                tcm = dve.do(lambda e: e.tensor_scalar(xc_[:, ci, :, h, :], csr[:, ci, :].rearrange("p (f n) -> p f n", f=8),
                                                       part[:, 1 + h:2 + h], 1.0 if ci == 0 else -1.0, ALU.mult, ALU.mult),
                             t_bc, t_hot, tfree)
            yield
        for ci in range(2):
            a, b, op = ((bre, bim, ALU.subtract), (bim, bre, ALU.add))[ci]
            tz = dve.do(lambda e: e.memset(fv(15360, 1024), 0.0), tfree, prev, tcm)
            t1 = dve.do(lambda e: e.tensor_tensor(m_[:, 0], a, bc(fr), ALU.mult), t_f[0], t_bc)
            t2 = dve.do(lambda e: e.tensor_tensor(m_[:, 1], b, bc(fi), ALU.mult))
            yield
            for h in range(2):
                hs = slice(64 * h, 64 * h + 64)
                tb = dve.do(lambda e: e.tensor_tensor(xh[hs, :, h, :], m_[hs, 0], m_[hs, 1], op), t1, t2, tz)
            yield
            for half in range(2):
                bank = 5 + half
                for j in range(4):
                    tt = pe.do(lambda e: e.transpose(PS[:, bank, j * P:j * P + P], xh2[:, 4 * half + j, :], ident[:, :]), tb, mfree[bank])
                prev = tt
                d = lb[:, ci, 4 * half:4 * half + 4, :]
                t = act.do(lambda e: e.copy(d, PS[:, bank, :].rearrange("p (a n) -> p a n", a=4)), tt, tfree)
                mfree[bank] = [t]
                t_lc.append(t)
                yield
        for ci in range(2):
            for half in range(2):
                bank = 5 + half
                for j in range(4):
                    tt = pe.do(lambda e: e.transpose(PS[:, bank, j * P:j * P + P], ct[:, ci, 4 * half + j, :], ident[:, :]), tcm, mfree[bank])
                d = ct[:, ci, 4 * half:4 * half + 4, :]
                t = act.do(lambda e: e.copy(d, PS[:, bank, :].rearrange("p (a n) -> p a n", a=4)), tt)
                mfree[bank] = [t]
                t_lc.append(t)
                yield
        done["matrices"] = t

    tt = pe.do(lambda e: e.matmul(PS[0:8, 5, 0:384], relb[0:32, :], hot[0:32, :], start=True, stop=True), t_hot)
    t1 = dve.do(lambda e: e.tensor_tensor(negr[0:8, :], PS[0:8, 5, 0:384], negr[0:8, :], ALU.add), tt)
    t_bs = dma(pool, [(scr_b, negr[0:8, :])], t1)
    mfree[5] = [t1]

    wada = w2("w_ada")
    aacc = sb("aacc", [P, 1024])
    waitfor, done = {}, {}
    ada_prev = [None, None]
    ada_open = set()
    busy = set()

    def ada_use(g, q, kt):
        def use(r, tok):
            w = g if g < 2 else 0
            a = aacc[:, :] if w == 0 else fv(U, 1024)
            if kt == 0:
                while w in ada_open:
                    step()
                t = dve.do(lambda e: e.tensor_scalar(a, r, cact[:, 0:1], None, ALU.mult), tok, t_c, ada_prev[w])
            else:
                t = dve.do(lambda e: e.scalar_tensor_tensor(a, r, cact[:, kt:kt + 1], a, ALU.mult, ALU.add), tok, ada_prev[w])
            ada_prev[w] = t
            if kt == 15:
                ada_open.add(w)
                background.append(ada_close(g, q, w, a))
            return t
        return use

    def ada_close(g, q, w, a, bank=7):
        o = g * 16 + q * 8
        for half in range(2):
            while bank in busy:
                yield
            for j in range(4):
                t = pe.do(lambda e: e.transpose(PS[:, bank, j * P:j * P + P], a[:, (4 * half + j) * P:(4 * half + j + 1) * P], ident[:, :]),
                          ada_prev[w], mfree[bank], t_small)
            m = mod[:, o + 4 * half:o + 4 * half + 4]
            t2 = dve.do(lambda e: e.tensor_reduce(m, PS[:, bank, :].rearrange("p (j n) -> p j n", j=4), AX, ALU.add), t)
            mfree[bank] = [t2]
            yield
        ada_prev[w] = t2
        ada_open.discard(w)
        yield
        done["mod%d%d" % (g, q)] = dve.do(lambda e: e.tensor_tensor(mod[:, o:o + 8], mod[:, o:o + 8], cols[:, C_BADA + o:C_BADA + o + 8],
                                                                    ALU.add), t2, t_cols[1])

    def row_use(q, kt):
        def use(r, tok):
            for half in range(2):
                t = pe.do(lambda e: e.matmul(PS[0:1, 2 * q + half, :], cact[:, kt:kt + 1], r[:, half * 512:half * 512 + 512],
                                             start=(kt == 0), stop=(kt == 15)), tok, t_c)
            if kt == 15:
                background.append(row_close(q, t))
            return t
        return use

    row_prev = [None]

    def row_close(q, t):
        row = aacc[0:1, :]
        a = act.do(lambda e: e.copy(row, PS[0:1, 2 * q:2 * q + 2, :].rearrange("p a n -> p (a n)")), t, row_prev[0])
        gfree[q] = [a]
        yield
        for j in range(8):
            t = pe.do(lambda e: e.matmul(PS[:, 7, j:j + 1], aacc[0:1, j * P:j * P + P], ones[0:1, 0:1], start=True, stop=True),
                      a, t_one, mfree[7])
        row_prev[0] = t
        o = q * 8
        t = dve.do(lambda e: e.tensor_tensor(mod[:, o:o + 8], PS[:, 7, 0:8], cols[:, C_BADA + o:C_BADA + o + 8], ALU.add), t, t_cols[1])
        mfree[7] = [t]
        done["mod0%d" % q] = t
        ada_prev[0] = t

    gfree[:] = ["busy", "busy"]
    for q in range(2):
        for kt in range(16):
            for g in (1, 0):
                c0 = g * D + q * 1024
                add_ada(wada[kt * P:(kt + 1) * P, c0:c0 + 1024].rearrange("p (k n) -> p k n", k=1),
                        ada_use(g, q, kt) if g else row_use(q, kt))

    def add_ada_group(g, q):
        for kt in range(16):
            c0 = g * D + q * 1024
            yield (wada[kt * P:(kt + 1) * P, c0:c0 + 1024].rearrange("p (k n) -> p k n", k=1), ada_use(g, q, kt))

    tmp = f3(3072, 3)
    tmpf = [None, None, None]

    sqt = fv(2048, 1024)
    ssf = {"t": None, "sq": None, "use": None}

    def add_squares(src, p, *tokens):
        a = act.do(lambda e: e.activation(sqt, src, ACT.Square), ssf["sq"], *tokens)
        yield
        sum_squares(p, a)

    def sum_squares(p, a):
        v = sqt.rearrange("p (k n) -> p n k", k=4)
        if p == 0:
            t = dve.do(lambda e: e.tensor_reduce(ss[:, :], v, AX, ALU.add), a, ssf["use"])
        else:
            t = dve.do(lambda e: e.tensor_reduce(tmp[:, 0, :], v, AX, ALU.add), a, tmpf[0])
            t = dve.do(lambda e: e.tensor_tensor(ss[:, :], ss[:, :], tmp[:, 0, :], ALU.add), t, ssf["t"])
            tmpf[0] = t
        ssf["sq"] = t
        ssf["t"] = t

    h = Operand(0, 1)
    yg = Operand(2)
    ys = Operand(0)
    ya = Operand(3)
    mg = Operand(1, 2)
    h2 = Operand(0, 3)
    hid = Operand(1, 2)

    w_in = w2("w_in")
    u3 = f3(U, 8)

    def ev_copy(dst, name, eng="act"):
        def ev(full, t):
            if eng == "act":
                r = act.do(lambda e: e.copy(dst, full), t, *waitfor.get(name, []))
            else:
                r = dve.do(lambda e: e.tensor_copy(dst, full), t, *waitfor.get(name, []))
            done[name] = r
            yield r
        return ev

    def ev_tanh(dst, name):
        def ev(full, t):
            r = act.do(lambda e: e.activation(dst, full, ACT.Tanh, scale=0.5), t, *waitfor.get(name, []))
            done[name] = r
            yield r
        return ev

    wA = F[:, SW:SW + 512].rearrange("p (c n) -> p c n", c=2)
    zz_ = [F[:, SW + 512 * i:SW + 512 * i + 512].rearrange("p (c n) -> p c n", c=2) for i in (1, 2)]
    sv_ = [F[:, SW + 512 * i:SW + 512 * i + 512].rearrange("p (c n) -> p c n", c=2) for i in (3, 4)]
    ptmp = fv(SW + 2560, 512)
    ptmp2 = ptmp.rearrange("p (c n) -> p c n", c=2)
    ptmp4 = ptmp.rearrange("p (k n) -> p k n", k=4)
    ebase = [E0, E0 + 2048, GB + 2048, GB, E0, E0 + 2048, GB + 2048, E0]
    after = {4: 0, 5: 1, 6: 2, 7: 4}
    e_ready, e_free = {}, {}

    def etable(ft):
        return f3(ebase[ft], 4), f3(ebase[ft] + 1024, 4)

    def make_e(ft):
        Ec, Es = etable(ft)
        w0 = e_free[after[ft]] if ft in after else [t_bs, tx[-1], t_cols[-1], t_hot] if ft in (0, 1) else [tx[-1], t_cols[-1]]
        tt = ft * 4
        t = pool.do(lambda e: e.memset(Ec[:, :, 0:1], 1.0), w0)
        t = pool.do(lambda e: e.memset(Es[:, :, 0:1], 0.0))
        t = pool.do(lambda e: e.tensor_copy(Ec[:, :, 1:2], ec[:, tt:tt + 4].unsqueeze(2)), t, t_e)
        t = pool.do(lambda e: e.tensor_copy(Es[:, :, 1:2], es[:, tt:tt + 4].unsqueeze(2)), t)
        n = 1
        while n < T:
            src, dst, cnt = 1, n + 1, min(n, T - 1 - n)
            cn, sn = (v[:, :, n:n + 1].broadcast_to([P, 4, cnt]) for v in (Ec, Es))
            c0, s0 = Ec[:, :, src:src + cnt], Es[:, :, src:src + cnt]
            c1, s1 = Ec[:, :, dst:dst + cnt], Es[:, :, dst:dst + cnt]
            A = ptmp4[:, :, 0:cnt]
            if cnt >= 31 and ft >= 4:
                for j in range(4):
                    ta = act.do(lambda e: e.activation(c1[:, j, :], c0[:, j, :], ACT.Copy, scale=Ec[:, j, n:n + 1]), t)
                    ta = act.do(lambda e: e.activation(s1[:, j, :], c0[:, j, :], ACT.Copy, scale=Es[:, j, n:n + 1]), t)
                yield
                t1 = pool.do(lambda e: e.tensor_tensor(A, s0, sn, ALU.mult), t, (pool.sem, pool.n))
                t2 = pool.do(lambda e: e.tensor_tensor(c1, c1, A, ALU.subtract), t1, ta)
                t1 = pool.do(lambda e: e.tensor_tensor(A, s0, cn, ALU.mult), t2)
                t = pool.do(lambda e: e.tensor_tensor(s1, s1, A, ALU.add), t1)
            else:
                t1 = pool.do(lambda e: e.tensor_tensor(A, s0, sn, ALU.mult), t, (pool.sem, pool.n))
                t2 = pool.do(lambda e: e.tensor_tensor(c1, c0, cn, ALU.mult), t)
                t3 = pool.do(lambda e: e.tensor_tensor(c1, c1, A, ALU.subtract), t1, t2)
                t4 = pool.do(lambda e: e.tensor_tensor(A, c0, sn, ALU.mult), t3)
                t5 = pool.do(lambda e: e.tensor_tensor(s1, s0, cn, ALU.mult), t3)
                t = pool.do(lambda e: e.tensor_tensor(s1, s1, A, ALU.add), t4, t5)
            n *= 2
            yield
        e_ready[ft] = t

    sfree = [None, None]
    zfree = [None, None]

    def gelu_task(ft, yb, ty):
        v, g1_ = ss[:, :], rstd[:, :]
        z1 = dve.do(lambda e: e.scalar_tensor_tensor(v, u3[:, ft, :], cols[:, C_SD + ft:C_SD + ft + 1], PS[:, yb, 0:T], ALU.mult, ALU.add),
                    ty, gf_[0])
        mfree[yb] = [z1]
        busy.discard(yb)
        yield
        z2 = act.do(lambda e: e.activation(g1_, v, ACT.Square), z1, gf_[0])
        yield
        z3 = dve.do(lambda e: e.tensor_scalar(g1_, g1_, GELU_A, 1.0, ALU.mult, ALU.add), z2)
        z4 = dve.do(lambda e: e.tensor_tensor(g1_, g1_, v, ALU.mult), z3)
        yield
        z5 = act.do(lambda e: e.activation(g1_, g1_, ACT.Tanh, scale=GELU_C), z4)
        yield
        z6 = dve.do(lambda e: e.scalar_tensor_tensor(v, g1_, 1.0, v, ALU.add, ALU.mult), z5)
        yield
        a = hi_out(yg, ft, 1, v, 0.5, z6)
        yield
        gf_[0] = lo_out(yg, ft, 1, v, 0.5, a)
        done["yg%d" % ft] = gf_[0]

    gf_ = [None]

    def ssm_task():
        tb_, xt, pt_ = {}, {}, {}
        while "matrices" not in done:
            yield
        gf_[0] = (dve.sem, dve.n)
        for i in range(36):
            if i < 32:
                ft, j = i // 4, i % 4
                while "u%d" % (ft // 4) not in done:
                    yield
                bank, rs = 4 + i % 2, slice(32 * j, 32 * j + 32)
                for ci in range(2):
                    tb_[i] = pe.do(lambda e: e.matmul(PS[:, bank, ci * T:ci * T + T], lb[rs, ci, ft, :], u3[rs, ft, :],
                                                      start=True, stop=True), mfree[bank], done["u%d" % (ft // 4)], t_lc)
            k = i - 1
            if 0 <= k < 32:
                ft, j, bank = k // 4, k % 4, 4 + k % 2
                while ft not in e_ready:
                    yield
                Ec, Es = etable(ft)
                cc, sn = Ec[:, j, :], Es[:, j, :]
                z = zz_[k % 2]
                bu = PS[:, bank, :].rearrange("p (c n) -> p c n", c=2)
                x1 = dve.do(lambda e: e.tensor_tensor(wA, bu, cc.unsqueeze(1).broadcast_to([P, 2, T]), ALU.mult), tb_[k], e_ready[ft],
                            xt.get(k - 1))
                dve.do(lambda e: e.tensor_tensor(z[:, 0, :], bu[:, 1, :], sn, ALU.mult), zfree[k % 2])
                x3 = dve.do(lambda e: e.tensor_tensor(z[:, 1, :], bu[:, 0, :], sn, ALU.mult))
                mfree[bank] = [x3]
            m = i - 2
            if 0 <= m < 32:
                ft = m // 4
                Ec, Es = etable(ft)
                ccb, snb = (v[:, m % 4, :].unsqueeze(1).broadcast_to([P, 2, T]) for v in (Ec, Es))
                s_, z_ = sv_[m % 2], zz_[m % 2]
                y1 = pool.do(lambda e: e.tensor_tensor(s_, z_, ccb, ALU.mult), xt[m], sfree[m % 2])
                y2 = pool.do(lambda e: e.tensor_tensor(ptmp2, z_, snb, ALU.mult), (pool.sem, pool.n))
                y3 = pool.do(lambda e: e.tensor_tensor(s_[:, 0, :], s_[:, 0, :], ptmp2[:, 1, :], ALU.subtract), y1, y2)
                pt_[m] = pool.do(lambda e: e.tensor_tensor(s_[:, 1, :], s_[:, 1, :], ptmp2[:, 0, :], ALU.add), y1, y2)
                zfree[m % 2] = y2
                if m % 4 == 3:
                    e_free[ft] = [y2]
            yield
            if 0 <= k < 32:
                x4 = dve.do(lambda e: e.tensor_tensor(wA[:, 0, :], wA[:, 0, :], z[:, 0, :], ALU.add), x3)
                x5 = dve.do(lambda e: e.tensor_tensor(wA[:, 1, :], wA[:, 1, :], z[:, 1, :], ALU.subtract))
                dec = mag[:, k:k + 1].broadcast_to([P, T])
                dve.do(lambda e: e.tensor_tensor_scan(z[:, 0, :], dec, wA[:, 0, :], 0.0, ALU.mult, ALU.add), x4)
                xt[k] = dve.do(lambda e: e.tensor_tensor_scan(z[:, 1, :], dec, wA[:, 1, :], 0.0, ALU.mult, ALU.add), x5)
            r = i - 3
            if 0 <= r < 32:
                ft, j = r // 4, r % 4
                yb = 6 + ft % 2
                busy.add(yb)
                for ci in range(2):
                    ty = pe.do(lambda e: e.matmul(PS[32 * j:32 * j + 32, yb, 0:T], ct[:, ci, ft, 32 * j:32 * j + 32], sv_[r % 2][:, ci, :],
                                                  start=(ci == 0), stop=(ci == 1)), pt_[r], mfree[yb])
                sfree[r % 2] = ty
                if j == 3:
                    background.append(gelu_task(ft, yb, ty))
            yield
        while "yg7" not in done:
            yield
        done["ssm"] = ty

    def e_task():
        for ft in range(8):
            while ft in after and after[ft] not in e_free:
                yield
            yield from make_e(ft)

    q3, k3, v3 = f3(Q, 8), f3(K, 8), f3(V, 8)
    bh = f3(BH, 8)
    awv = F[:, AW:AW + 3 * 772].rearrange("p (r n) -> p r n", r=3)
    vn = f3(U, 2, 1024)
    SCALE1 = 128.0 ** -0.5
    atf = [None, None, None]

    def attn_head(hd, t_b):
        r = hd % 3
        w = awv[:, r, :]
        s_, pt = w[:, 0:384], w[:, 384:768]
        mx, sm = w[:, 768:770], w[:, 770:772]
        ba = 4 + r
        tq = [done["q%d" % (hd // 4)], done["k%d" % (hd // 4)]]
        p1 = pe.do(lambda e: e.matmul(PS[:, ba, 0:256], q3[:, hd, 128:256], k3[:, hd, :], start=True, stop=True), tq, mfree[ba])
        p1 = pe.do(lambda e: e.matmul(PS[:, ba, 256:384], q3[:, hd, 0:128], k3[:, hd, 0:128], start=True, stop=True))
        yield
        d1 = dve.do(lambda e: e.scalar_tensor_tensor(s_[:, 0:256], PS[:, ba, 0:256], SCALE1, bh[:, hd, :], ALU.mult, ALU.add), p1, t_b, atf[r])
        d2 = dve.do(lambda e: e.scalar_tensor_tensor(s_[:, 256:384], PS[:, ba, 256:384], SCALE1, bh[:, hd, 128:256], ALU.mult, ALU.add))
        d3 = dve.do(lambda e: e.tensor_reduce(mx[:, 0:1], s_[:, 0:256], AX, ALU.max, negate=True), d1)
        d4 = dve.do(lambda e: e.tensor_reduce(mx[:, 1:2], s_[:, 256:384], AX, ALU.max, negate=True), d2)
        yield
        a1 = act.do(lambda e: e.activation(s_[:, 0:256], s_[:, 0:256], ACT.Exp, bias=mx[:, 0:1], accum_out=sm[:, 0:1]), d3)
        a2 = act.do(lambda e: e.activation(s_[:, 256:384], s_[:, 256:384], ACT.Exp, bias=mx[:, 1:2], accum_out=sm[:, 1:2]), d4)
        yield
        d5 = dve.do(lambda e: e.reciprocal(sm, sm), a1, a2)
        d6 = dve.do(lambda e: e.tensor_scalar(s_[:, 0:256], s_[:, 0:256], sm[:, 0:1], None, ALU.mult), d5)
        d7 = dve.do(lambda e: e.tensor_scalar(s_[:, 256:384], s_[:, 256:384], sm[:, 1:2], None, ALU.mult), d5)
        yield
        yield
        for src, dst in ((256, 0), (0, 128), (128, 256)):
            p3 = pe.do(lambda e, src=src, dst=dst: e.transpose(PS[:, ba, dst:dst + P], s_[:, src:src + P], ident[:, :]), d6, d7)
        a3 = act.do(lambda e: e.copy(pt, PS[:, ba, 0:384]), p3)
        yield
        yield
        vh = slice(hd * P, hd * P + P)
        pe.quiet(lambda e: e.matmul(PS[:, ba, 0:256], vn[:, 0, vh], pt[:, 0:256], start=True, stop=False, skip_group_check=True), a3, done["vn%d" % (hd // 4)])
        p4 = pe.do(lambda e: e.matmul(PS[:, ba, 128:256], vn[:, 1, vh], pt[:, 256:384], start=False, stop=True, skip_group_check=True))
        atf[r] = p4
        yield
        t = split_out(ya, hd, 1, PS[:, ba, 0:256], 1.0, p4)
        mfree[ba] = [t]

    h_free = [None]
    tbias = [None]

    def attn_task():
        for i in range(10):
            yield
        for i in range(4):
            bank = 4 + i % 2
            t = pe.do(lambda e: e.matmul(PS[:, bank, :], fv(AW + 2320, P), fv(AW + i * 512, 512), start=True, stop=True),
                      tbias[0], mfree[bank])
            t = act.do(lambda e: e.copy(fv(BH + i * 512, 512), PS[:, bank, :]), t)
            mfree[bank] = [t]
        t_b = t
        atf[0] = atf[1] = atf[2] = t
        gl["x"] = [gl["x"], t]
        background.extend([heads_task(r, t_b) for r in range(3)])
        for g in range(2):
            while "v%d" % g not in done:
                yield
            for i in range(2):
                for hd in range(4 * g, 4 * g + 4):
                    t = pe.do(lambda e, i=i, hd=hd: e.transpose(PS[:, 7, (hd % 4) * P:(hd % 4) * P + P], v3[:, hd, i * P:i * P + P],
                                                                ident[:, :]), done["v%d" % g], mfree[7])
                t = act.do(lambda e, i=i, g=g: e.copy(vn[:, i, g * 512:g * 512 + 512], PS[:, 7, :]), t)
                mfree[7] = [t]
                yield
            done["vn%d" % g] = t

    def heads_task(r, t_b):
        for i in range(3 * r):
            yield
        for hd in range(r, 8, 3):
            while "vn%d" % (hd // 4) not in done:
                yield
            yield from attn_head(hd, t_b)
            yield
        done["att1%d" % r] = True

    runs = []

    def panel(W, k0, nkt, c0, operand, evac):
        srcs, mms = std(W, k0, nkt, c0)
        p = add_panel(srcs, 2, mms, operand, evac)
        runs.append(p)
        return p

    def call(f):
        runs.append(f)

    def all_done():
        return [(x.sem, x.n) for x in (pe, act, dve, pool)]

    X3 = f3(XT, 16)

    def norm1():
        for q in range(2):
            while "mod0%d" % q not in done or "mod1%d" % q not in done or t_ss[0] is None or t_xs[0] is None:
                yield
            s8 = slice(8 * q, 8 * q + 8)
            t = dve.do(lambda e: e.scalar_tensor_tensor(A1[:, s8], mod[:, 16 + 8 * q:24 + 8 * q], 1.0, cols[:, C_G1 + 8 * q:C_G1 + 8 * q + 8],
                                                        ALU.add, ALU.mult), done["mod1%d" % q], t_cols[0])
            tx_, tb = {}, {}
            for n in range(6):
                ks = lambda n: (8 * q + 2 * n, 8 * q + 2 * n + 1)
                if n < 4:
                    for k in ks(n):
                        tx_[k] = dve.do(lambda e: e.scalar_tensor_tensor(X3[:, k, :], X3[:, k, :], A1[:, k:k + 1], rstd[:, :], ALU.mult, ALU.mult),
                                        t, t_ss[0], t_xs[0])
                if 0 < n < 5:
                    for k in ks(n - 1):
                        tb[k] = act.do(lambda e: e.activation(h.hi(k), X3[:, k, :], ACT.Identity, bias=mod[:, k:k + 1]), tx_[k], done["mod0%d" % q])
                if n > 1:
                    for k in ks(n - 2):
                        h.ready[k] = dve.do(lambda e: e.scalar_tensor_tensor(h.lo(k), X3[:, k, :], mod[:, k:k + 1], h.hi(k).bitcast(F32),
                                                                             ALU.add, ALU.subtract), tb[k])
                if q == 0:
                    yield
        waitfor["ga0"] = [h.ready[15], t_xs[0]]
        waitfor["u0"] = [done["mod01"], done["mod11"], (pe.sem, pe.n)]
        background.append(ssm_task())
        done["h"] = t

    def start():
        background.extend([x_task(), param_task(), e_task(), norm1()])
        for j in range(64):
            advance(j)
            step()
            if j == 30:
                background.append(matrix_task())

    call(start)

    def ev_u0(full, t):
        drain("h")
        yield from ev_copy(fv(U, 1024), "u0")(full, t)

    for p in range(2):
        panel(w_in, 0, 16, p * 512, h, ev_copy(fv(U + p * 1024, 1024), "u%d" % p) if p else ev_u0)
    for i in range(4):
        panel(w_in, 0, 16, 4096 + i * 512, h, ev_tanh(fv(GA + i * 1024, 1024), "ga%d" % i))

    def table_gone(ft, name):
        while ft not in e_free:
            step()
        waitfor[name] = e_free[ft]

    for i in range(4):
        if i == 0:
            call(lambda: table_gone(3, "gb0"))
        if i == 2:
            call(lambda: table_gone(6, "gb2"))
        panel(w_in, 0, 16, 6144 + i * 512, h, ev_tanh(fv(GB + i * 1024, 1024), "gb%d" % i))

    GLT = 20880

    def ssm_end():
        drain("ssm")
        free = all_done()
        waitfor["q0"] = waitfor["v0"] = waitfor["k0"] = free
        pairs = [(fv(AW + 2320, P), I["c_swap"][:, P:2 * P])]
        for hd in range(8):
            src = bass.AP(tensor=scr_b.tensor, offset=scr_b.offset + hd * 384, ap=[[1, P], [1, T]])
            pairs.append((fv(AW + hd * T, T), src))
        tbias[0] = dma(pool, pairs, t_bs, free)
        gl["x"] = free
        background.append(attn_task())

    gl = {"x": None}

    def ev_q0(full, t):
        ssm_end()
        yield from ev_copy(fv(Q, 1024), "q0")(full, t)

    for i in range(2):
        for nm, cb, dst in (("q", 1024, Q), ("k", 2048, K), ("v", 3072, V)):
            panel(w_in, 0, 16, cb + i * 512, h, ev_q0 if nm + str(i) == "q0" else ev_copy(fv(dst + i * 1024, 1024), "%s%d" % (nm, i)))

    def after_w_in():
        h_free[0] = (pe.sem, pe.n)

    call(after_w_in)

    def ev_glu(p):
        def ev(full, t):
            tmp_ = fv(GLT, 512)
            for m in range(4):
                k = 4 * p + m
                a = act.do(lambda e: e.activation(full[:, m * T:m * T + T], full[:, m * T:m * T + T], ACT.Tanh, scale=0.5, bias=hbg[:, k:k + 1]), t)
            for half in range(2):
                f = full[:, half * 512:half * 512 + 512]
                k = 4 * p + 2 * half
                b = dve.do(lambda e: e.tensor_tensor(tmp_, yg.hi(k, 2).bitcast(F32), yg.lo(k, 2).bitcast(F32), ALU.add), gl["x"])
                b = dve.do(lambda e: e.scalar_tensor_tensor(f, f, 1.0, tmp_, ALU.add, ALU.mult), a, b)
                gl["x"] = b
                a2 = hi_out(ys, k, 2, f, 0.5, b, h_free[0])
            yc = lo_out(ys, 4 * p, 4, full, 0.5, a2)
            yield yc
        return ev

    w_glu = w2("w_glu")
    for p in range(2):
        panel(w_glu, 0, 8, p * 512, yg, ev_glu(p))

    def after_glu():
        mg_free[0] = [(pe.sem, pe.n), gl["x"]]

    mg_free = [None]
    call(after_glu)

    def ev_gate1(off, name):
        def ev(full, t):
            g = fv(off, 1024)
            r = dve.do(lambda e: e.scalar_tensor_tensor(g, g, 1.0, full, ALU.add, ALU.mult), t)
            done[name] = r
            yield r
        return ev

    def ev_gate2(off, off1, op, k, name, free):
        def ev(full, t):
            g = fv(off, 1024)
            r = dve.do(lambda e: e.scalar_tensor_tensor(g, g, 1.0, full, ALU.add, ALU.mult), t)
            r2 = dve.do(lambda e: e.tensor_tensor(g, g, fv(off1, 1024), ALU.add), r)
            yield r
            a = hi_out(op, k, 4, g, 0.5, r2, *free())
            yield
            lo_out(op, k, 4, g, 0.5, a)
        return ev

    wps, wpa = w2("w_proj_ssm"), w2("w_proj_attn")
    for i in range(4):
        panel(wps, 0, 8, i * 512, ys, ev_gate1(GA + i * 1024, "ps%d" % i))

    XR = 10240
    xr3 = f3(XR, 16)
    t_x2 = [None]

    def reload_x():
        drain("att10", "att11", "att12")
        t_x2[0] = dma(pool, [(fv(XR, 4096), scr_x)], t_xs[0], all_done())

    for i in range(4):
        panel(wpa, 0, 8, i * 512, ya, ev_gate2(GB + i * 1024, GA + i * 1024, mg, 4 * i, "pa%d" % i, lambda: mg_free[0]))

    def ev_res(dst3, p, gcol, need, final=True, then=None):
        def ev(full, t):
            for m in range(4):
                k = 4 * p + m
                r = dve.do(lambda e, k=k, m=m: e.scalar_tensor_tensor(dst3[:, k, :], full[:, m * T:m * T + T], gcol[:, k:k + 1],
                                                                     dst3[:, k, :], ALU.mult, ALU.add), t, t_x2[0], done[need])
            yield r
            if final:
                yield from add_squares(dst3[:, 4 * p:4 * p + 4, :].rearrange("p k n -> p (k n)"), p, r)
            if then:
                yield from then(p, r)
        return ev

    w_out = w2("w_out")
    call(reload_x)


    def warm_sqrt():
        act.do(lambda e: e.activation(der[:, 14, 1:2], eps[:, 0:1], ACT.Sqrt), t_eps)

    def count_out(i):
        def then(p, r):
            done["w_out%d" % i] = ssf["t"]
            yield
        return then

    for i in range(4):
        if i == 3:
            call(warm_sqrt)
        panel(w_out, 0, 16, i * 512, mg, ev_res(xr3, i, mod[:, 32:48], "mod21", True, count_out(i)))

    def norm2(free):
        while "w_out3" not in done:
            yield
        t = dve.do(lambda e: e.scalar_tensor_tensor(A2, mod[:, 64:80], 1.0, cols[:, C_GM:C_GM + 16], ALU.add, ALU.mult),
                   done["mod40"], done["mod41"])
        ts = stats(4, ssf["t"], mfree[4])
        mfree[4] = [ts]
        ssf["use"] = ts
        slot = lambda q: fv(2048 + (q % 6) * T, T)
        ta, tb = {}, {}
        for n in range(10):
            if n < 8:
                for q in (2 * n, 2 * n + 1):
                    ta[q] = dve.do(lambda e: e.scalar_tensor_tensor(slot(q), xr3[:, q, :], A2[:, q:q + 1], rstd[:, :], ALU.mult, ALU.mult),
                                   t, ts, tmpf, ssf["sq"], h2.ready[q - 6] if q > 5 else None)
            if 0 < n < 9:
                for q in (2 * n - 2, 2 * n - 1):
                    tb[q] = act.do(lambda e: e.activation(h2.hi(q), slot(q), ACT.Identity, bias=mod[:, 48 + q:49 + q]), ta[q], free,
                                   done["mod30"], done["mod31"])
            if n > 1:
                for q in (2 * n - 4, 2 * n - 3):
                    h2.ready[q] = dve.do(lambda e: e.scalar_tensor_tensor(h2.lo(q), slot(q), mod[:, 48 + q:49 + q], h2.hi(q).bitcast(F32),
                                                                          ALU.add, ALU.subtract), tb[q])
            if n > 1:
                yield
        tmpf[:] = [h2.ready[15]] * 3
        ssf["sq"] = h2.ready[15]
        done["h2"] = True

    call(lambda: background.append(norm2((pe.sem, pe.n))))

    def ffn(W1, W2, src, hid, ev2, tag):
        for ch in range(4):
            def fresh():
                hidf[0] = (pe.sem, pe.n)
                hid.ready[:] = [None] * 16
            call(fresh)
            for i in range(4):
                def ev(full, t, i=i):
                    r = ffr[:, i % 2, :]
                    a = act.do(lambda e: e.activation(r, full, ACT.Relu), t, fff[i % 2])
                    yield a
                    b = dve.do(lambda e: e.tensor_tensor(r, r, r, ALU.mult), a)
                    yield
                    c = hi_out(hid, 4 * i, 4, r, 1.0, b, hidf[0])
                    yield
                    fff[i % 2] = lo_out(hid, 4 * i, 4, r, 1.0, c)
                panel(W1, 0, 16, ch * 2048 + i * 512, src, ev)
            if ch == 3:
                call(hu_free)
            for i in range(4):
                panel(W2, ch * 16, 16, i * 512, hid, ev2(ch, i))

    FFR = 0
    ffr = F[:, FFR:FFR + 2048].rearrange("p (r n) -> p r n", r=2)
    fff = [None, None]
    hidf = [None]
    call(lambda: background.append(rope_task()))
    HU = Operand(0, 3)
    ss2, r1 = fv(8960, 256), fv(8704, 256)
    gfc, gfp = cols[:, C_GF:C_GF + 16], dcol(15)
    tgf = dve.do(lambda e: e.tensor_tensor(gfp, gfc, cols[:, C_PRE:C_PRE + 16], ALU.mult), t_cols[1])
    n3 = {"t": None}

    def before_norm3(p, tok):
        yield
        for m in range(4):
            k = 4 * p + m
            a = act.do(lambda e: e.activation(HU.hi(k), xr3[:, k, :], ACT.Copy, scale=gfp[:, k:k + 1]), tok, tgf, n3["pe"])
            b = dve.do(lambda e: e.scalar_tensor_tensor(HU.lo(k), xr3[:, k, :], gfp[:, k:k + 1], HU.hi(k).bitcast(F32), ALU.mult, ALU.subtract), a)
            HU.ready[k] = b
            if m == 1:
                yield
        yield
        for m in range(4):
            k = 4 * p + m
            a = act.do(lambda e: e.activation(sqt[:, m * T:m * T + T], xr3[:, k, :], ACT.Square, scale=gfc[:, k:k + 1]), tok, ssf["sq"], t_cols[1])
        yield
        v = sqt.rearrange("p (k n) -> p n k", k=4)
        if p == 0:
            t = dve.do(lambda e: e.tensor_reduce(ss2, v, AX, ALU.add), a)
        else:
            t = dve.do(lambda e: e.tensor_reduce(tmp[:, 0, :], v, AX, ALU.add), a, tmpf[0])
            t = dve.do(lambda e: e.tensor_tensor(ss2, ss2, tmp[:, 0, :], ALU.add), t, n3["t"])
            tmpf[0] = t
        ssf["sq"] = t
        n3["t"] = t
        done["S2%d" % p] = t

    def hu_free():
        n3["pe"] = (pe.sem, pe.n)

    ffn(w2("w_ff1"), w2("w_ff2"), h2, hid, lambda ch, i: ev_res(xr3, i, mod[:, 80:96], "mod51", ch == 3, before_norm3 if ch == 3 else None), "1")

    H = Operand(1, 2)
    xc = Operand(0, 3)
    YA = Operand(0, 3)
    MG = Operand(1, 2)
    H2 = Operand(0, 3)
    HID = Operand(1, 2)
    XC = 0
    Q2 = 4096
    KK = 14336
    VN = 15360
    VT = 18432
    ROT = 16384
    W8 = 18432
    cosb, sinb, nz, zz = (fv(ROT + i * 256, 256) for i in range(4))
    AWK = ROT + 1024
    invf = part[:, 0:1]
    msk = fv(8192, 256)
    swp = fv(8448, 128)
    sink = fv(8576, 32)
    rot = {}

    def rope_task():
        pos = sinb.bitcast(I32)
        free = [(pe.sem, pe.n), (dve.sem, dve.n), (act.sem, act.n), (pool.sem, pool.n)]
        t = dma(pool, [(pos, I["positions_2"][0:1, :].broadcast_to([P, T])),
                       (msk, I["c_mask"]), (swp, I["c_swap"][:, 0:P]),
                       (sink, I["attn_sinks_2"][0:1, :].broadcast_to([P, 32]))], *free)
        for i in range(6):
            yield
        rot["sink"] = t
        pf = zz
        kk = nz
        t1 = dve.do(lambda e: e.tensor_copy(pf, pos), t, *free)
        t1 = dve.do(lambda e: e.tensor_scalar(sinb, pf, invf, None, ALU.mult), t1)
        t1 = reduce_angle(sinb, kk, t1)
        yield
        t2 = act.do(lambda e: e.activation(cosb, sinb, ACT.Sin, scale=0.5), t1)
        t2 = act.do(lambda e: e.activation(sinb, sinb, ACT.Sin), t2)
        t3 = dve.do(lambda e: e.tensor_tensor(cosb, cosb, cosb, ALU.mult), t2)
        t3 = dve.do(lambda e: e.tensor_scalar(cosb, cosb, -2.0, 1.0, ALU.mult, ALU.add), t3)
        t4 = dve.do(lambda e: e.tensor_scalar(nz, pf, 0.0, None, ALU.not_equal), t1)
        t4 = dve.do(lambda e: e.tensor_scalar(zz, pf, 0.0, None, ALU.is_equal), t4)
        rot["t"] = [t3, t4]
        warm_sqrt()
        yield


    rsum = {}

    def norm3(free):
        while "S23" not in done:
            yield
        t = dve.do(lambda e: e.scalar_tensor_tensor(ss2, ss[:, :], 1e-6, ss2, ALU.mult, ALU.add), n3["t"], ssf["t"])
        yield
        u = pe.do(lambda e: e.matmul(PS[:, 4, 0:T], ones[:, :], ss2, start=True, stop=True), t_one, t, mfree[4])
        u1 = pe.do(lambda e: e.matmul(PS[:, 5, 0:T], ones[:, :], ss[:, :], start=True, stop=True), ssf["t"], mfree[5])
        yield
        a = act.do(lambda e: e.activation(rstd[:, :], PS[:, 4, 0:T], ACT.Sqrt, scale=1.0 / D, bias=eps2), u, t_e2, ssf["t"])
        a1 = act.do(lambda e: e.activation(r1, PS[:, 5, 0:T], ACT.Sqrt, scale=1.0 / D, bias=eps[:, 0:1]), u1)
        mfree[4], mfree[5] = [a], [a1]
        ssf["use"] = u1
        trs = dve.do(lambda e: e.reciprocal(rstd[:, :], rstd[:, :]), a)
        done["rs"] = trs
        yield
        slot = lambda q: fv(2048 + (q % 6) * T, T)
        sfr, tb = {}, {}
        for n in range(10):
            if n < 8:
                for q in (2 * n, 2 * n + 1):
                    a = dve.do(lambda e: e.scalar_tensor_tensor(slot(q), xr3[:, q, :], gfp[:, q:q + 1], rstd[:, :], ALU.mult, ALU.mult),
                               trs, tmpf, ssf["sq"], H.ready[q - 6] if q > 5 else None)
                    sfr[q] = a
            if 0 < n < 9:
                for q in (2 * n - 2, 2 * n - 1):
                    tb[q] = act.do(lambda e: e.activation(H.hi(q), slot(q), ACT.Copy), sfr[q], free)
            if n > 1:
                for q in (2 * n - 4, 2 * n - 3):
                    t = dve.do(lambda e: e.tensor_tensor(H.lo(q), slot(q), H.hi(q).bitcast(F32), ALU.subtract), tb[q])
                    H.ready[q] = t
            yield
        tmpf[:] = [t, t, t]
        ssf["sq"] = t
        done["H"] = t
        t1 = dve.do(lambda e: e.reciprocal(r1, r1), a1)
        while "O15" not in done:
            yield
        for k in range(16):
            t = dve.do(lambda e: e.scalar_tensor_tensor(xr3[:, k, :], xr3[:, k, :], gfc[:, k:k + 1], r1, ALU.mult, ALU.mult), t1)
            if k % 2:
                yield
        done["y"] = t

    call(lambda: background.append(norm3((pe.sem, pe.n))))
    win2 = w2("w_in_2")
    xc3 = f3(XC, 16)
    cw = lambda w, k: cols[:, C_CW + 16 * w + k:C_CW + 16 * w + k + 1]

    def ev_conv(p):
        def ev(full, t):
            if p < 2:
                drain("rs")
                f3_ = full.rearrange("p (k n) -> p k n", k=4)
                t = dve.do(lambda e: e.tensor_tensor(f3_, f3_, rstd[:, :].unsqueeze(1).broadcast_to([P, 4, T]), ALU.mult), t, done["rs"])
            if p > 1:
                drain("H")
            for m in range(4):
                k = 4 * p + m
                a = act.do(lambda e, k=k, m=m: e.activation(xc3[:, k, :], full[:, m * T:m * T + T], ACT.Identity, scale=cw(3, k),
                                                            bias=cols[:, C_CB + k:C_CB + k + 1]), t, fff, done.get("H"))
            a0 = a
            yield
            for m in range(4):
                if m == 2:
                    yield
                k = 4 * p + m
                pm = full[:, m * T:m * T + T]
                y = xc3[:, k, :]
                a = a0
                for d in (1, 2, 3):
                    r = dve.do(lambda e, k=k, d=d, pm=pm, y=y: e.scalar_tensor_tensor(y[:, d:T], pm[:, 0:T - d], cw(3 - d, k), y[:, d:T],
                                                                                     ALU.mult, ALU.add), a)
                    a = r
            yield r
            while "hu" not in done:
                yield
            a = hi_out(xc, 4 * p, 4, fv(XC + 1024 * p, 1024), 1.0, r, done["hu"])
            yield
            lo_out(xc, 4 * p, 4, fv(XC + 1024 * p, 1024), 1.0, a)
        return ev

    for i in range(4):
        panel(win2, 0, 16, i * 512, H if i > 1 else HU, ev_conv(i))
        if i == 1:
            call(lambda: done.update(hu=(pe.sem, pe.n)))

    GW = 16384 + 1024
    gA = fv(GW, 1024)
    gM = fv(GW + 1024, 1024)
    gX = fv(GW + 2048, 1024)
    gT = {"x": None}

    def rg_panel(name, p, ev):
        v = I[name].rearrange("o b (k p) j -> p (o b k) j", p=P)
        srcs = [v[:, 4 * p:4 * p + 4, :]]
        mms = lambda u: [(b * 512 + kk * 256 + jt * P, 4 * p + 2 * b + kk, 2 * b + jt)
                         for b in range(2) for jt in range(2) for kk in range(2)]
        x = add_panel(srcs, 4, mms, xc, ev)
        runs.append(x)

    def ev_ra(p):
        def ev(full, t):
            for m in range(4):
                k = 4 * p + m
                a = act.do(lambda e: e.activation(gA[:, m * T:m * T + T], full[:, m * T:m * T + T], ACT.Tanh, scale=0.5,
                                                  bias=hba[:, k:k + 1]), t, gT["x"])
            yield a
            for m in range(4):
                k = 4 * p + m
                o = gA[:, m * T:m * T + T]
                b = dve.do(lambda e: e.tensor_scalar(o, o, 1.0, spc[:, k:k + 1], ALU.add, ALU.mult), a, t_sp[0])
            yield
            c1 = act.do(lambda e: e.activation(gM, gA, ACT.Tanh, scale=-1.0), b, gT["x"])
            c2 = act.do(lambda e: e.activation(gA, gA, ACT.Exp), b)
            c4 = act.do(lambda e: e.activation(gX, gA, ACT.Square), c2, gT["x"])
            yield
            d1 = dve.do(lambda e: e.scalar_tensor_tensor(gM, gX, 1.0, gM, ALU.add, ALU.mult), c1, c4)
            nb = lambda v: v.unsqueeze(1).broadcast_to([P, 4, T])
            g3 = lambda v: v.rearrange("p (k n) -> p k n", k=4)
            d2 = dve.do(lambda e: e.tensor_tensor(g3(gA), g3(gA), nb(nz), ALU.mult), c2, c4, rot["t"])
            gT["r"] = d1
            yield
            c3 = act.do(lambda e: e.activation(gM, gM, ACT.Sqrt), d1)
            yield
            d3 = dve.do(lambda e: e.tensor_tensor(g3(gM), g3(gM), nb(nz), ALU.mult), c3)
            d4 = dve.do(lambda e: e.tensor_tensor(g3(gM), g3(gM), nb(zz), ALU.add), d3)
            gT["m"] = [d2, d4]
            done["ra%d" % p] = d4
        return ev

    def ev_rx(p):
        def ev(full, t):
            for m in range(4):
                k = 4 * p + m
                a = act.do(lambda e: e.activation(gX[:, m * T:m * T + T], full[:, m * T:m * T + T], ACT.Tanh, scale=0.5,
                                                  bias=hbx[:, k:k + 1]), t, gT["r"])
            yield a
            xv = fv(XC + 1024 * p, 1024)
            b = dve.do(lambda e: e.scalar_tensor_tensor(gX, gX, 1.0, xv, ALU.add, ALU.mult), a)
            b = dve.do(lambda e: e.scalar_tensor_tensor(gX, gX, 0.5, gM, ALU.mult, ALU.mult), b, gT["m"])
            yield
            for m in range(4):
                k = 4 * p + m
                sl = slice(m * T, m * T + T)
                c = dve.do(lambda e: e.tensor_tensor_scan(xc3[:, k, :], gA[:, sl], gX[:, sl], 0.0, ALU.mult, ALU.add), b)
            gT["x"] = c
            done["scan%d" % p] = c
        return ev

    yt = {"x": None}

    def ev_yr(p):
        def ev(full, t):
            g, y = gY, fv(AWK2, 1024)
            a0 = act.do(lambda e: e.copy(y, full), t, yt["x"])
            a = act.do(lambda e: e.activation(g, full, ACT.Square), t, yt["x"])
            yield a
            b = dve.do(lambda e: e.tensor_scalar(g, g, GELU_A, 1.0, ALU.mult, ALU.add), a)
            b = dve.do(lambda e: e.tensor_tensor(g, g, y, ALU.mult), b, a0)
            yield
            c = act.do(lambda e: e.activation(g, g, ACT.Tanh, scale=GELU_C), b)
            yield
            d = dve.do(lambda e: e.scalar_tensor_tensor(g, g, 1.0, y, ALU.add, ALU.mult), c)
            d2 = dve.do(lambda e: e.scalar_tensor_tensor(g, g, 0.5, fv(XC + 1024 * p, 1024), ALU.mult, ALU.mult), d, done["scan%d" % p])
            yield
            a = hi_out(xc, 4 * p, 4, g, 1.0, d2, rgdone[p])
            yield
            yt["x"] = lo_out(xc, 4 * p, 4, g, 1.0, a)
            done["yr%d" % p] = yt["x"]
        return ev

    AWK2 = 20480
    gY = fv(9216, 1024)
    rgdone = {}
    qtmp = fv(KK, 1024)
    qt_ = {"x": None}

    def rope(dst, n, a, qtmp):
        for m in range(n):
            bank = 4 + m // 2
            b = pe.do(lambda e: e.matmul(PS[:, bank, (m % 2) * T:(m % 2) * T + T], swp, dst[:, m * T:m * T + T],
                                         start=True, stop=True), a, mfree[4], mfree[5], rot["sink"])
        yield
        nb = lambda v: v.unsqueeze(1).broadcast_to([P, n, T])
        d3 = dst.rearrange("p (k n) -> p k n", k=n)
        t3 = qtmp.rearrange("p (k n) -> p k n", k=n)
        sw3 = PS[:, 4:6, :].rearrange("p a n -> p (a n)")[:, 0:n * T].rearrange("p (k n) -> p k n", k=n)
        c = dve.do(lambda e: e.tensor_tensor(t3, sw3, nb(sinb), ALU.mult), b, qt_["x"], rot["t"])
        mfree[4] = mfree[5] = [c]
        d = dve.do(lambda e: e.tensor_tensor(d3, d3, nb(cosb), ALU.mult), b)
        yield
        qt_["x"] = dve.do(lambda e: e.tensor_tensor(d3, d3, t3, ALU.add), c, d)

    def EVQ(i):
        def ev(full, t):
            dst = fv(Q2 + 1024 * i, 1024)
            a = act.do(lambda e: e.copy(dst, full), t)
            yield a
            yield from rope(dst, 4, a, qtmp)
            done["Q%d" % i] = qt_["x"]
        return ev

    def EVKV(full, t):
        kt_ = fv(VT + 512, 512)
        a = act.do(lambda e: e.copy(kt_, full[:, 0:512]), t, gT["x"])
        a2 = act.do(lambda e: e.copy(fv(VT, 512), full[:, 512:1024]), t)
        yield a2
        yield from rope(kt_, 2, a, fv(15872, 512))
        for j in range(4):
            src = kt_[64 * (j % 2):64 * (j % 2) + 64, (j // 2) * T:(j // 2) * T + T]
            for half in range(2):
                c = dve.do(lambda e: e.tensor_copy(F[64 * half:64 * half + 64, KK + j * T:KK + j * T + T], src), qt_["x"])
        done["K"] = c
        yield
        for m in range(2):
            for i in range(2):
                b = pe.do(lambda e: e.transpose(PS[:, 6, i * T + m * P:i * T + m * P + P], fv(VT + m * T + i * P, P), ident[:, :]),
                          a2, mfree[6])
        yield
        v = act.do(lambda e: e.copy(fv(VN, 512), PS[:, 6, :]), b, qt_["x"])
        mfree[6] = [v]
        done["V"] = v


    def after_rg(i):
        rgdone[i] = (pe.sem, pe.n)

    for i in range(4):
        if i:
            call(lambda i=i: drain("scan%d" % (i - 1)))
        rg_panel("w_rg_a_2", i, ev_ra(i))
        panel(win2, 0, 16, 4096 + i * 512, H, EVQ(i))
        call(lambda i=i: drain("ra%d" % i))
        rg_panel("w_rg_x_2", i, ev_rx(i))
        call(lambda i=i: after_rg(i))
        panel(win2, 0, 16, 2048 + i * 512, H, ev_yr(i))
    call(lambda: drain("scan3", "Q3"))
    panel(win2, 0, 16, 6144, H, EVKV)

    aw2 = F[:, 17408:17408 + 2 * 1600].rearrange("p (r n) -> p r n", r=2)
    af2 = [None, None]

    def before_heads():
        drain("V", "yr3")
        af2[0] = af2[1] = all_done()


    def head2(pr, r):
        kv = pr // 4
        w = aw2[:, r, :]
        s_ = w[:, 0:768]
        pt = w[:, 768:1536]
        mx, sm, es_ = w[:, 1536:1540], w[:, 1540:1544], w[:, 1544:1548]
        ba = (4, 5) if r == 0 else (6, 7)
        qt = Q2 + pr * T
        tq = [done["Q%d" % (pr // 4)], done["K"]]
        for x in range(2):
            hs = slice(64 * x, 64 * x + 64)
            pe.do(lambda e, x=x, hs=hs: e.matmul(PS[:, ba[x], 0:256], F[hs, qt + 128:qt + 256], F[hs, KK + kv * T:KK + kv * T + T],
                                                 start=True, stop=True), tq, mfree[ba[x]])
            p1 = pe.do(lambda e, x=x, hs=hs: e.matmul(PS[:, ba[x], 256:384], F[hs, qt:qt + 128], F[hs, KK + kv * T:KK + kv * T + P],
                                                      start=True, stop=True))
        yield
        for x in range(2):
            o = x * 384
            d1 = dve.do(lambda e, x=x, o=o: e.scalar_tensor_tensor(s_[:, o:o + 256], PS[:, ba[x], 0:256], 0.125, msk, ALU.mult, ALU.add), p1, af2[r])
            d1 = dve.do(lambda e, x=x, o=o: e.scalar_tensor_tensor(s_[:, o + 256:o + 384], PS[:, ba[x], 256:384], 0.125, msk[:, 128:256], ALU.mult, ALU.add))
        for x in range(2):
            o = x * 384
            dve.do(lambda e, x=x, o=o: e.tensor_reduce(mx[:, 2 * x:2 * x + 1], s_[:, o:o + 256], AX, ALU.max), d1)
            d2 = dve.do(lambda e, x=x, o=o: e.tensor_reduce(mx[:, 2 * x + 1:2 * x + 2], s_[:, o + 256:o + 384], AX, ALU.max))
        skb = sink[:, 2 * pr:2 * pr + 2].unsqueeze(2).broadcast_to([P, 2, 2])
        v2 = lambda v: v.rearrange("p (a b) -> p a b", a=2)
        d3 = dve.do(lambda e: e.tensor_tensor(v2(mx), v2(mx), skb, ALU.max), d2)
        d4 = dve.do(lambda e: e.tensor_tensor(v2(es_), skb, v2(mx), ALU.subtract), d3)
        d5 = dve.do(lambda e: e.tensor_scalar(mx, mx, -1.0, None, ALU.mult), d4)
        yield
        a0 = act.do(lambda e: e.activation(es_, es_, ACT.Exp), d4)
        for x in range(2):
            o = x * 384
            act.do(lambda e, x=x, o=o: e.activation(s_[:, o:o + 256], s_[:, o:o + 256], ACT.Exp, bias=mx[:, 2 * x:2 * x + 1], accum_out=sm[:, 2 * x:2 * x + 1]), d5)
            a1 = act.do(lambda e, x=x, o=o: e.activation(s_[:, o + 256:o + 384], s_[:, o + 256:o + 384], ACT.Exp, bias=mx[:, 2 * x + 1:2 * x + 2], accum_out=sm[:, 2 * x + 1:2 * x + 2]))
        yield
        d6 = dve.do(lambda e: e.tensor_tensor(sm, sm, es_, ALU.add), a1)
        d7 = dve.do(lambda e: e.reciprocal(sm, sm), d6)
        for x in range(2):
            o = x * 384
            dve.do(lambda e, x=x, o=o: e.tensor_scalar(s_[:, o:o + 256], s_[:, o:o + 256], sm[:, 2 * x:2 * x + 1], None, ALU.mult), d7)
            d8 = dve.do(lambda e, x=x, o=o: e.tensor_scalar(s_[:, o + 256:o + 384], s_[:, o + 256:o + 384], sm[:, 2 * x + 1:2 * x + 2], None, ALU.mult))
        yield
        for x in range(2):
            o = x * 384
            for src, dst in ((256, 0), (0, 128), (128, 256)):
                p3 = pe.do(lambda e, x=x, o=o, src=src, dst=dst: e.transpose(PS[:, ba[x], dst:dst + P], s_[:, o + src:o + src + P], ident[:, :]), d8)
        yield
        for x in range(2):
            a3 = act.do(lambda e, x=x: e.copy(pt[:, x * 384:x * 384 + 384], PS[:, ba[x], 0:384]), p3)
        yield
        for x in range(2):
            hs = slice(64 * x, 64 * x + 64)
            o = x * 384
            pe.do(lambda e, hs=hs, o=o: e.matmul(PS[hs, ba[0], 0:256], fv(VN + kv * 64, 64), pt[:, o:o + 256], start=True, stop=False,
                                                 skip_group_check=True), a3, done["V"])
            p4 = pe.do(lambda e, hs=hs, o=o: e.matmul(PS[hs, ba[0], 128:256], fv(VN + 256 + kv * 64, 64), pt[:, o + 256:o + 384],
                                                      start=False, stop=True, skip_group_check=True))
        af2[r] = p4
        yield
        t = act.do(lambda e: e.copy(fv(qt, 256), PS[:, ba[0], 0:256]), p4)
        mfree[ba[0]] = [t]
        mfree[ba[1]] = [t]
        done["O%d" % pr] = t

    def attn2_task(r):
        for i in range(4 * r):
            yield
        for pr in range(r, 16, 2):
            yield from head2(pr, r)
            yield

    call(before_heads)
    call(lambda: background.extend([attn2_task(0), attn2_task(1)]))
    G1 = 0
    def wait_scan():
        waitfor["gr0"] = [yt["x"]]

    call(wait_scan)
    for i in range(4):
        panel(win2, 0, 16, 6656 + i * 512, H, ev_tanh(fv(i * 1024, 1024), "gr%d" % i))

    wrp, wap = w2("w_rnn_proj_2"), w2("w_attn_proj_2")
    for i in range(4):
        panel(wrp, 0, 16, i * 512, xc, ev_gate1(i * 1024, "rp%d" % i))

    def convert_att():
        tf = (pe.sem, pe.n)
        def task():
            for i in range(4):
                while "O%d" % (4 * i + 3) not in done or "O%d" % (4 * i + 2) not in done:
                    yield
                a = hi_out(YA, 4 * i, 4, fv(Q2 + 1024 * i, 1024), 1.0, done["O%d" % (4 * i + 3)], done["O%d" % (4 * i + 2)], tf)
                yield
                lo_out(YA, 4 * i, 4, fv(Q2 + 1024 * i, 1024), 1.0, a)
        background.append(task())

    call(convert_att)

    def heads_done():
        drain("O14", "O15")
        waitfor["gt0"] = [(pe.sem, pe.n), (dve.sem, dve.n), (act.sem, act.n)]

    GT = 14336
    for i in range(4):
        if i == 0:
            call(heads_done)
        panel(win2, 0, 16, 8704 + i * 512, H, ev_tanh(fv(GT + i * 1024, 1024), "gt%d" % i))

    mgf = [None]

    def att_ready():
        mgf[0] = (pe.sem, pe.n)

    call(att_ready)
    for i in range(4):
        panel(wap, 0, 16, i * 512, YA, ev_gate2(GT + i * 1024, i * 1024, MG, 4 * i, "ap%d" % i, lambda: [mgf[0]]))
    O = 4096
    O3 = f3(O, 16)
    wo2 = w2("w_out_2")

    def ev_o(p, ch, last):
        def ev(full, t):
            o = fv(O + 1024 * p, 1024)
            if ch == 0:
                r = dve.do(lambda e: e.tensor_copy(o, full), t, onorm[0])
            else:
                r = dve.do(lambda e: e.tensor_tensor(o, o, full, ALU.add), t, onorm[0])
            yield r
            if last:
                yield from add_squares(o, p, r)
        return ev

    onorm = [None]

    def before_o():
        onorm[0] = [(act.sem, act.n), (dve.sem, dve.n)]

    call(before_o)
    gpo = cols[:, C_POST:C_POST + 16]

    def ev_wo(p):
        def ev(full, t):
            a = act.do(lambda e: e.activation(sqt, full, ACT.Square), ssf["sq"], t)
            for m in range(4):
                k = 4 * p + m
                b = act.do(lambda e: e.activation(O3[:, k, :], full[:, m * T:m * T + T], ACT.Copy, scale=gpo[:, k:k + 1]), onorm[0])
            yield b
            sum_squares(p, a)
            done["wo%d" % p] = b
        return ev

    for i in range(4):
        if i == 3:
            call(warm_sqrt)
        panel(wo2, 0, 16, i * 512, MG, ev_wo(i))

    gmp = cols[:, C_MPRE:C_MPRE + 16]
    rs2, rs4 = fv(8704, 256), fv(8960, 256)

    def norm4(free):
        while "wo3" not in done or "y" not in done:
            yield
        ts = stats(4, ssf["t"], mfree[4])
        mfree[4] = [ts]
        ssf["use"] = ts
        xa, ha = {}, {}

        def scaled(p):
            o = f3(O + 1024 * p, 4)
            return dve.do(lambda e: e.tensor_tensor(o, o, rstd[:, :].unsqueeze(1).broadcast_to([P, 4, T]), ALU.mult), ts, done["wo%d" % p])

        def added(p, t):
            xa[p] = pool.do(lambda e: e.tensor_tensor(fv(XR + 1024 * p, 1024), fv(XR + 1024 * p, 1024), fv(O + 1024 * p, 1024), ALU.add), t, done["y"])

        def high(p):
            for k in range(4 * p, 4 * p + 4):
                ha[p] = act.do(lambda e: e.activation(H2.hi(k), xr3[:, k, :], ACT.Copy, scale=gmp[:, k:k + 1]), xa[p], free)

        def low(p):
            for k in range(4 * p, 4 * p + 4):
                H2.ready[k] = dve.do(lambda e: e.scalar_tensor_tensor(H2.lo(k), xr3[:, k, :], gmp[:, k:k + 1], H2.hi(k).bitcast(F32),
                                                                      ALU.mult, ALU.subtract), ha[p])

        for k in range(4):
            t = dve.do(lambda e: e.tensor_tensor(O3[:, k, :], O3[:, k, :], rstd[:, :], ALU.mult), ts, done["wo0"])
            t = dve.do(lambda e: e.tensor_tensor(xr3[:, k, :], xr3[:, k, :], O3[:, k, :], ALU.add), t, done["y"])
            a = act.do(lambda e: e.activation(H2.hi(k), xr3[:, k, :], ACT.Copy, scale=gmp[:, k:k + 1]), t, free)
            ha[0] = a
        xa[0] = t
        added(1, scaled(1))
        low(0)
        added(2, scaled(2))
        yield
        high(1)
        yield
        low(1)
        high(2)
        t = scaled(3)
        added(3, t)
        yield
        low(2)
        yield
        high(3)
        yield
        low(3)
        onorm[0] = [t, xa[3]]
        for p in range(4):
            yield
            yield from add_squares(fv(XR + 1024 * p, 1024), p, xa[p])
        yield
        u = pe.do(lambda e: e.matmul(PS[:, 4, 0:T], ones[:, :], ss[:, :], start=True, stop=True), ssf["t"], mfree[4])
        ssf["use"] = u
        yield
        t = dve.do(lambda e: e.tensor_scalar(rs4, PS[:, 4, 0:T], 1.0 / D, 1e-6, ALU.mult, ALU.add), u)
        mfree[4] = [t]
        t = dve.do(lambda e: e.reciprocal(rs2, rs4), t)
        yield
        done["rs4"] = dve.do(lambda e: e.tensor_tensor(rs4, rs2, rs2, ALU.mult), t)

    call(lambda: background.append(norm4((pe.sem, pe.n))))
    ffn(w2("w_mlp_up_2"), w2("w_mlp_down_2"), H2, HID, lambda ch, i: ev_o(i, ch, ch == 3), "2")

    def finale():
        drain()
        t = pe.do(lambda e: e.matmul(PS[:, 4, 0:T], ones[:, :], ss[:, :], start=True, stop=True), ssf["t"], mfree[4])
        t = dve.do(lambda e: e.tensor_tensor(rstd[:, :], PS[:, 4, 0:T], rs4, ALU.mult), t, done["rs4"])
        t = act.do(lambda e: e.activation(rstd[:, :], rstd[:, :], ACT.Sqrt, scale=1.0 / D, bias=eps[:, 0:1]), t)
        t = dve.do(lambda e: e.reciprocal(rstd[:, :], rstd[:, :]), t)
        ts = dve.do(lambda e: e.tensor_tensor(rstd[:, :], rstd[:, :], rs2, ALU.mult), t)
        gp = cols[:, C_MPOST:C_MPOST + 16]
        yo = F[:, 14336:14336 + 4096].rearrange("p (i n) -> p i n", i=2)
        toks = []
        fr_ = [None, None]
        for p in range(8):
            for k in range(2 * p, 2 * p + 2):
                r = dve.do(lambda e, k=k: e.scalar_tensor_tensor(O3[:, k, :], O3[:, k, :], gp[:, k:k + 1], rstd[:, :], ALU.mult, ALU.mult), ts)
            add = pool if p % 2 else dve
            r = add.do(lambda e, p=p: e.tensor_tensor(fv(XR + 512 * p, 512), fv(XR + 512 * p, 512), fv(O + 512 * p, 512), ALU.add), r)
            bank = 4 + p % 4
            for i in range(2):
                for j in range(2):
                    k = 2 * p + j
                    tt = pe.do(lambda e, i=i, j=j, k=k, bank=bank: e.transpose(
                        PS[:, bank, i * T + j * P:i * T + j * P + P], xr3[:, k, i * P:i * P + P], ident[:, :]),
                        r, toks[p - 4] if p >= 4 else ts)
            toks.append(act.do(lambda e, p=p, bank=bank: e.copy(yo[:, :, 2 * p * P:2 * p * P + 256],
                                                                PS[:, bank, :].rearrange("p (i n) -> p i n", i=2)), tt, ts))
            if p % 4 == 3:
                c0 = (p // 4) * 1024
                fin.append(dma(sp, [(out[0, i * P:(i + 1) * P, c0:c0 + 1024], yo[:, i, c0:c0 + 1024]) for i in range(2)], toks[-1]))
        sp.wait(*fin)
        sp.wait(t_xs[0], t_bs)

    fin = []
    call(finale)

    ada_groups = [(2, 0), (2, 1), (3, 0), (3, 1), (4, 0), (4, 1), (5, 0), (5, 1)]
    first, rest = units[:64], units[64:]
    order = list(first)
    extra = []
    for g, q in ada_groups:
        for kt, (src, use) in enumerate(add_ada_group(g, q)):
            extra.append({"kind": "ada", "src": src, "nk": 1, "use": use})
    xs, ys_ = zip(*ADAP)
    DUE = lambda n: int(np.interp(n, xs, ys_))
    for n, u in enumerate(rest):
        order.append(u)
        due = DUE(n)
        while extra and 128 - len(extra) < due:
            order.append(extra.pop(0))
    assert not extra
    units[:] = order
    for j, u in enumerate(units):
        index_of[id(u)] = j
    wunits = [j for j, u in enumerate(units) if u["kind"] == "w"]
    for n, j in enumerate(wunits):
        ahead[j] = wunits[min(n + LOOK, len(wunits) - 1)]
    for j in range(RAWN):
        send(j)
    for item in runs:
        if isinstance(item, Panel):
            run_panel(item)
        else:
            item()


_OUT = (1, 256, 2048)


def kernel(**inputs):
    import concourse.bacc as bacc
    from concourse.bass_utils import run_bass_kernel_spmd

    nc = bacc.Bacc("TRN2", target_bir_lowering=False, num_devices=1)
    arrays, aps = {}, {}
    for name, a in list(inputs.items()) + list(constants().items()):
        a = np.ascontiguousarray(a)
        arrays["in_" + name] = a
        aps[name] = nc.dram_tensor("in_" + name, a.shape, mybir.dt.from_np(a.dtype), kind="ExternalInput").ap()
    out = nc.dram_tensor("out_0", _OUT, F32, kind="ExternalOutput").ap()
    scr_x = nc.dram_tensor("scr_x", (P, 4096), F32, kind="Internal").ap()
    scr_b = nc.dram_tensor("scr_b", (8, 384), F32, kind="Internal").ap()
    build(nc, aps, out, scr_x, scr_b)
    r = run_bass_kernel_spmd(nc, [arrays], core_ids=[0])
    return r.results[0]["out_0"]
```
